# Optimizing a Trainium2 kernel written in Bass

```python
import math
import jax, jax.numpy as jnp
from jax import lax
import numpy as np

D_MODEL = 1024
BATCH = 1
SEQ = 512
DEPTH = 1

HGRN_HEADS = 4
HGRN_DK = 128
HGRN_DV = 128
HGRN_WIDTH = HGRN_HEADS * HGRN_DV
HGRN_CHUNK = 64

ATT_HEADS = 8
ATT_DH = 64
ATT_WIDTH = ATT_HEADS * ATT_DH
IDX_HEADS = 8
IDX_DIM = 64
TOPK_MAX = 256
Q_BLOCK = 128

N_BUCKETS = 32
MAX_DISTANCE = 128

MIX_WIDTH = HGRN_WIDTH + ATT_WIDTH
FFN_HIDDEN = -(-8 * D_MODEL // (3 * 256)) * 256
EPS = 1e-6

PROJ_SIZES = (HGRN_HEADS * HGRN_DK,
              HGRN_HEADS * HGRN_DK,
              HGRN_WIDTH,
              HGRN_WIDTH,
              ATT_WIDTH,
              ATT_WIDTH,
              ATT_WIDTH,
              IDX_HEADS * IDX_DIM,
              IDX_DIM,
              IDX_HEADS)
PROJ_TOTAL = sum(PROJ_SIZES)
PROJ_SPLITS = tuple(int(v) for v in np.cumsum(PROJ_SIZES)[:-1])

kernel_name = "hymba_hgrn2_dsa_sandwich_block"

def rmsnorm(x, gain):
    xf = x.astype(jnp.float32)
    xf = xf * lax.rsqrt(jnp.mean(xf * xf, axis=-1, keepdims=True) + EPS)
    return (xf * gain.astype(jnp.float32)).astype(x.dtype)

def hgrn2_mixer(q, f_logit, i, g, lb, gnorm):
    B, S, _ = q.shape
    C = HGRN_CHUNK
    nc = S // C
    f32 = jnp.float32
    qf = jax.nn.silu(q.astype(f32))
    f = lb + (1.0 - lb) * jax.nn.sigmoid(f_logit.astype(f32))
    log_f = jnp.log(f)
    kf = 1.0 - f
    vf = i.astype(f32)

    def to_chunks(t, d):
        return t.reshape(B, nc, C, HGRN_HEADS, d).transpose(1, 0, 3, 2, 4)

    xs = (to_chunks(qf, HGRN_DK), to_chunks(kf, HGRN_DK),
          to_chunks(vf, HGRN_DV), to_chunks(log_f, HGRN_DK))
    causal = jnp.tril(jnp.ones((C, C), dtype=bool))[None, None, :, :, None]

    def step(state, chunk):
        qb, kb, vb, gb = chunk
        b = jnp.cumsum(gb, axis=2)
        diff = b[:, :, :, None, :] - b[:, :, None, :, :]
        decay = jnp.exp(jnp.where(causal, diff, -jnp.inf))
        scores = jnp.einsum('bhtk,bhtsk,bhsk->bhts', qb, decay, kb)
        o = (jnp.einsum('bhts,bhsv->bhtv', scores, vb)
             + jnp.einsum('bhtk,bhkv->bhtv', qb * jnp.exp(b), state))
        b_last = b[:, :, -1:, :]
        new_state = (jnp.exp(b_last[:, :, 0, :])[..., None] * state
                     + jnp.einsum('bhsk,bhsv->bhkv', kb * jnp.exp(b_last - b), vb))
        return new_state, o

    s0 = jnp.zeros((B, HGRN_HEADS, HGRN_DK, HGRN_DV), f32)
    _, o = lax.scan(step, s0, xs)
    o = o.transpose(1, 0, 3, 2, 4).reshape(B, S, HGRN_HEADS, HGRN_DV)
    o = rmsnorm(o, gnorm).reshape(B, S, HGRN_WIDTH)
    return (o * jax.nn.silu(g.astype(f32))).astype(q.dtype)

def t5_bucket(n):
    n = jnp.maximum(n, 0)
    max_exact = N_BUCKETS // 2
    nf = jnp.maximum(n, 1).astype(jnp.float32)
    large = max_exact + (jnp.log(nf / max_exact) / math.log(MAX_DISTANCE / max_exact)
                         * (N_BUCKETS - max_exact)).astype(jnp.int32)
    large = jnp.minimum(large, N_BUCKETS - 1)
    return jnp.where(n < max_exact, n, large)

def dsa_mixer(q, k, v, q_idx, k_idx, w_idx, rel_bias):
    B, S = q.shape[0], q.shape[1]
    top = min(TOPK_MAX, S // 4)
    nb = S // Q_BLOCK
    f32 = jnp.float32
    scale = ATT_DH ** -0.5
    k_idx32 = k_idx.astype(f32) * (IDX_DIM ** -0.5)
    w32 = w_idx.astype(f32) * (IDX_HEADS ** -0.5)
    bias_tab = rel_bias.astype(f32)
    key_pos = jnp.arange(S, dtype=jnp.int32)
    gather = jax.vmap(lambda src, idx: src[idx])

    def blocks(t):
        return t.reshape((B, nb, Q_BLOCK) + t.shape[2:]).swapaxes(0, 1)

    def one_block(xs):
        qb, qib, wb, blk = xs
        qpos = blk * Q_BLOCK + jnp.arange(Q_BLOCK, dtype=jnp.int32)
        causal = key_pos[None, :] <= qpos[:, None]
        dots = jnp.einsum('bqhd,bsd->bqhs', qib.astype(f32), k_idx32)
        score = jnp.einsum('bqh,bqhs->bqs', wb, jax.nn.relu(dots))
        score = jnp.where(causal[None], score, -jnp.inf)
        _, sel = lax.top_k(score, top)
        k_sel = gather(k, sel)
        v_sel = gather(v, sel)
        dist = qpos[None, :, None] - sel
        bias = bias_tab[t5_bucket(dist)]
        logits = (jnp.einsum('bqhd,bqkhd->bqhk', qb, k_sel).astype(f32) * scale
                  + bias.transpose(0, 1, 3, 2))
        logits = jnp.where((dist >= 0)[:, :, None, :], logits, -jnp.inf)
        p = jax.nn.softmax(logits, axis=-1)
        return jnp.einsum('bqhk,bqkhd->bqhd', p.astype(v.dtype), v_sel)

    out = lax.map(one_block, (blocks(q), blocks(q_idx), blocks(w32),
                              jnp.arange(nb, dtype=jnp.int32)))
    return out.swapaxes(0, 1).reshape(B, S, ATT_WIDTH)

def setup_inputs(seed: int = 0) -> dict:
    key = jax.random.key(seed)
    ks = jax.random.split(key, 14)
    f32 = jnp.float32
    n = lambda k, shape, s: jax.random.normal(k, shape, f32) * s
    return {
        "x": n(ks[0], (BATCH, SEQ, D_MODEL), 1.0),
        "w_in": n(ks[1], (DEPTH, D_MODEL, PROJ_TOTAL), D_MODEL ** -0.5),
        "lb_logits": n(ks[2], (DEPTH + 1, HGRN_HEADS * HGRN_DK), 0.5),
        "hgrn_gnorm": 1.0 + n(ks[3], (DEPTH, HGRN_DV), 0.1),
        "rel_bias": n(ks[4], (N_BUCKETS, ATT_HEADS), 0.5),
        "w_o": n(ks[5], (DEPTH, MIX_WIDTH, D_MODEL), MIX_WIDTH ** -0.5),
        "norm_pre_mix": 1.0 + n(ks[6], (DEPTH, D_MODEL), 0.1),
        "norm_post_mix": 1.0 + n(ks[7], (DEPTH, D_MODEL), 0.1),
        "norm_pre_ffn": 1.0 + n(ks[8], (DEPTH, D_MODEL), 0.1),
        "norm_post_ffn": 1.0 + n(ks[9], (DEPTH, D_MODEL), 0.1),
        "w_gate": n(ks[10], (DEPTH, D_MODEL, FFN_HIDDEN), D_MODEL ** -0.5),
        "w_up": n(ks[11], (DEPTH, D_MODEL, FFN_HIDDEN), D_MODEL ** -0.5),
        "w_down": n(ks[12], (DEPTH, FFN_HIDDEN, D_MODEL), FFN_HIDDEN ** -0.5),
    }

def reference(x, w_in, lb_logits, hgrn_gnorm, rel_bias, w_o, norm_pre_mix, norm_post_mix,
              norm_pre_ffn, norm_post_ffn, w_gate, w_up, w_down):
    B, S, _ = x.shape
    lb_all = jnp.cumsum(jax.nn.softmax(lb_logits.astype(jnp.float32), axis=0), axis=0)
    for l in range(DEPTH):
        h = rmsnorm(x, norm_pre_mix[l])
        proj = jnp.einsum('bsd,de->bse', h, w_in[l])
        hq, hf, hi, hg, aq, ak, av, iq, ik, iw = jnp.split(proj, PROJ_SPLITS, axis=-1)
        y_a = hgrn2_mixer(hq, hf, hi, hg, lb_all[l], hgrn_gnorm[l])
        y_b = dsa_mixer(aq.reshape(B, S, ATT_HEADS, ATT_DH),
                        ak.reshape(B, S, ATT_HEADS, ATT_DH),
                        av.reshape(B, S, ATT_HEADS, ATT_DH),
                        iq.reshape(B, S, IDX_HEADS, IDX_DIM), ik, iw, rel_bias)
        y = jnp.einsum('bse,ed->bsd', jnp.concatenate([y_a, y_b.astype(y_a.dtype)], axis=-1), w_o[l])
        x = x + rmsnorm(y, norm_post_mix[l])
        h = rmsnorm(x, norm_pre_ffn[l])
        ff = jax.nn.silu(jnp.einsum('bsd,df->bsf', h, w_gate[l])) * jnp.einsum('bsd,df->bsf', h, w_up[l])
        ff = jnp.einsum('bsf,fd->bsd', ff, w_down[l])
        x = x + rmsnorm(ff, norm_post_ffn[l])
    return x


_drawn_inputs = setup_inputs


def setup_inputs(seed=0):
    import zlib

    import numpy as np

    out = dict(_drawn_inputs(seed))
    spreads = {}
    factors = {}
    for name, (base, spread) in spreads.items():
        noise = np.random.default_rng([zlib.crc32(name.encode()), seed]).standard_normal(out[name].shape)
        drawn = base * np.exp(spread * noise) if base else spread * noise
        out[name] = __import__('jax').numpy.asarray(drawn.astype(out[name].dtype))
    for name, factor in factors.items():
        out[name] = (out[name] * factor).astype(out[name].dtype)
    return out
```

```python
from contextlib import ExitStack

import numpy as np

import concourse.bass as bass
from concourse import mybir

P = 128
F32 = mybir.dt.float32
F32R = mybir.dt.float32r
U32 = mybir.dt.uint32
ALU = mybir.AluOpType
ACT = mybir.ActivationFunctionType
AX = mybir.AxisListType

HEADS_A, DK = 4, 128
HEADS_B, DH = 8, 64
TOPK_MAX = 256
N_BUCKETS, MAX_DISTANCE = 32, 128
EPS = 1e-6
FUTURE = -2.0e38
TAKEN = -3.0e38
CLOSED = -1.0e30


def bucket_onehot(seq):
    exact = N_BUCKETS // 2
    n = np.maximum(seq - 1 - np.arange(seq + P), 0)
    large = exact + (np.log(np.maximum(n, 1) / exact) / np.log(MAX_DISTANCE / exact)
                     * (N_BUCKETS - exact) + 1e-9).astype(np.int64)
    bucket = np.where(n < exact, n, np.minimum(large, N_BUCKETS - 1))
    return (np.arange(N_BUCKETS)[:, None] == bucket[None, :]).astype(np.float32)


def hymba_layer(nc, x, w_in, lb_logits, hgrn_gnorm, rel_bias, w_o, norm_pre_mix, norm_post_mix,
                norm_pre_ffn, norm_post_ffn, w_gate, w_up, w_down, onehot, out):
    _, S, D = x.shape
    F = w_gate.shape[2]
    TB = S // P
    KT = D // P
    FT = F // P
    W = HEADS_A * DK
    TOP = min(TOPK_MAX, S // 4)
    assert (S, D, W, TB, KT, FT, TOP) == (512, 1024, 512, 4, 8, 22, 128)
    CH = KT * 256

    x_d, out_d = x[0], out[0]
    wi, wo, wg, wu, wd = w_in[0], w_o[0], w_gate[0], w_up[0], w_down[0]
    gscr = nc.dram_tensor("bias_by_distance", [HEADS_B, P, S + P], F32, kind="Internal").ap()

    SEG = {"f": W, "q": 0, "i": 2 * W, "g": 3 * W, "aq": 4 * W, "ak": 5 * W, "av": 6 * W, "iq": 7 * W}
    chunks = [("iq", 0), ("iq", 1), ("ikw", 0)]
    chunks += [(s, c) for s in ("f", "q", "i", "g", "aq", "ak", "av") for c in range(2)]
    J_WO = len(chunks)
    chunks += [("wo", c) for c in range(KT // 2)]
    J_FF = len(chunks)
    for c in range(FT // 2):
        chunks += [("gate", c), ("up", c)]
    J_DN = len(chunks)
    chunks += [("down", c) for c in range(FT // 2)]
    NCH = len(chunks)
    IKW = DH + HEADS_B

    groups = []
    for j in range(J_WO):
        for m in range(1 if chunks[j][0] == "ikw" else 2):
            groups.append((j, chunks[j][0], chunks[j][1], m))
    first_group = {}
    for g, (j, kind, c, m) in enumerate(groups):
        first_group.setdefault(kind, g)

    LEVELS = [64, 32, 16, 8, 4, 2, 1]
    J_LEVEL = 7
    PAIRS = [(c, s) for c in range(TB) for s in range(c)]
    UNITS = TB * HEADS_B

    with ExitStack() as ctx:
        def sb(name, shape, dt=F32):
            return ctx.enter_context(nc.sbuf_tensor(name, shape, dt))

        def sem(name):
            return ctx.enter_context(nc.semaphore(name))

        PS = ctx.enter_context(nc.psum_tensor("PS", [P, 8, 512], F32))

        hT_hi = sb("hT_hi", [P, KT, S], F32R)
        hT_lo = sb("hT_lo", [P, KT, S], F32R)
        raw = sb("raw", [P, 2, CH])
        w_hi = sb("w_hi", [P, 2, CH], F32R)
        w_lo = sb("w_lo", [P, 2, CH], F32R)
        ident = sb("ident", [P, P])
        lmask = sb("lmask", [P, len(LEVELS), 64])
        M0 = sb("M0", [P, P])
        iw = sb("iw", [P, TB, HEADS_B])
        ss = sb("ss", [P, 40])
        ms = sb("ms", [P, 40])
        rstd = sb("rstd", [P, 40])
        mhalf = sb("mhalf", [P, 16])
        lbt = sb("lbt", [P, 2, HEADS_A])
        lbw = sb("lbw", [P, 6, HEADS_A])
        gn = sb("gn", [P, 1])
        eB = sb("eB", [P, HEADS_A, TB])
        top8 = sb("top8", [P, 8])
        mx = sb("mx", [P, UNITS])
        nm = sb("nm", [P, UNITS])
        sm = sb("sm", [P, UNITS])
        rs = sb("rs", [P, UNITS])

        N1, N2 = FT * 2 * S, 7936
        low = ExitStack()
        A1 = low.enter_context(nc.sbuf_tensor("A1", [P, N1], F32))
        low.close()
        ff = sb("ff", [P, FT, 2, S], F32R)
        A2 = sb("A2", [P, N2])

        def a1(o, n):
            return A1[:, o:o + n]

        V, gT, ya = a1(0, 2048), a1(2048, 2048), a1(4096, 2048)
        aqT, akT, av = a1(6144, 2048), a1(8192, 2048), a1(10240, 2048)
        iqT = aqT
        ikT, iwT = a1(10240, 512), a1(10752, 512)
        Z = [a1(12288, 2048), a1(14336, 2048)]
        xin = a1(12288, 4096).rearrange("p (t d) -> p t d", t=TB)
        Bh = a1(12288, 4096).rearrange("p (h c) -> p h c", h=HEADS_B)
        Sd = a1(16384, 2048).rearrange("p (c n) -> p c n", c=TB)
        So = a1(18432, 3072).rearrange("p (i n) -> p i n", i=len(PAIRS))
        gain_in = a1(16384, 1024)
        BM = [a1(16384 + 512 * i, 512) for i in range(3)]
        Pb = [a1(17920 + 512 * i, 512) for i in range(3)]
        PT = [a1(19456 + 512 * i, 512) for i in range(2)]
        scr = [a1(21504, 1024), a1(20480, 1024)]
        rl = [a1(21504, 512), a1(22016, 512)]
        UX, LX = a1(21504, 512), a1(22016, 512)
        qT, kT = A2[:, 0:2048], A2[:, 2048:4096]
        x2 = A2[:, 0:4096].rearrange("p (t d) -> p t d", t=TB)
        bT = A2[:, 4096:6144]
        oh_sb, tab, g_sb = A2[0:N_BUCKETS, 4096:4736], A2[0:N_BUCKETS, 4736:4744], A2[0:HEADS_B, 4768:5408]
        gain_mid = A2[:, 4096:6144].rearrange("p (a d) -> p a d", a=2)
        sig = [A2[:, 4096:4608], A2[:, 4608:5120]]
        fraw = [A2[:, 5120:5632], A2[:, 5632:6144]]
        SC = {1: A2[:, 6144:6400], 2: A2[:, 6400:6784], 3: A2[:, 6784:7296]}
        gain_out = A2[:, 6144:7168]
        junk = a1(16384, 1024)

        s_x = [sem(f"x_landed{t}") for t in range(TB)]
        s_gin = sem("gain_in_landed")
        s_small = sem("small_landed")
        s_raw = [sem(f"raw_landed{i}") for i in range(2)]
        s_hi = sem("w_hi_ready")
        s_lo = sem("w_lo_ready")
        s_rows = sem("row_chunk_used")
        s_ss = sem("sumsq_ready")
        s_rs = sem("rstd_ready")
        s_pool = sem("pool_chain")
        s_dve = sem("dve_chain")
        s_const = sem("const_ready")
        s_hx = sem("h_ready")
        s_hps = sem("hT_psum")
        s_hhi = sem("hT_hi_ready")
        s_hlo = sem("hT_lo_ready")
        s_proj = sem("proj_done")
        s_ev = [sem(f"proj_evacuated{b}") for b in range(4)]
        s_sig = sem("silu_sigmoid_ready")
        s_lbm = sem("lb_max_sub")
        s_lbe = sem("lb_exp")
        s_gps = sem("bias_row_psum")
        s_gsb = sem("bias_row_sbuf")
        s_gst = sem("bias_row_stored")
        s_bh = sem("bias_tile_landed")
        s_iwp = sem("w_idx_psum")
        s_iws = sem("w_idx_ready")
        s_dot = sem("idx_dots")
        s_rl = sem("idx_relu")
        s_sc = sem("idx_score")
        s_fut = sem("score_causal")
        s_mask = sem("mask_ready")
        s_f = sem("forget_ready")
        s_ln = sem("log_f_ready")
        s_b = sem("cumsum_ready")
        s_rst = sem("scan_reset_ready")
        s_D = sem("level_exponent")
        s_E = sem("level_exp")
        s_Z = sem("level_operands")
        s_lvl = sem("level_scores_psum")
        s_ma = sem("level_merged")
        s_eb = sem("chunk_decay")
        s_off = sem("offdiag_psum")
        s_ofs = sem("offdiag_sbuf")
        s_o = sem("hgrn_o_psum")
        s_half = sem("half_of_squares")
        s_ya = sem("hgrn_o_sbuf")
        s_yn = sem("hgrn_y_normed")
        s_yt = sem("hgrn_yT_psum")
        s_yg = sem("hgrn_yT_gated")
        s_bm = sem("bias_mask")
        s_qk = sem("logits_psum")
        s_nm = sem("neg_max")
        s_ex = sem("exp_done")
        s_pn = sem("probs_normed")
        s_ptp = sem("probsT_psum")
        s_pts = sem("probsT_sbuf")
        s_pv = sem("pv_done")
        s_yhi = sem("yT_hi_ready")
        s_ylo = sem("yT_lo_ready")
        s_mid = sem("x_and_gains_landed")
        s_wo = sem("mix_out_psum")
        s_pa = sem("mix_out_read")
        s_x2 = sem("x2_ready")
        s_gu = sem("gate_up_psum")
        s_fs = sem("gate_sigmoid")
        s_fr = sem("ff_raw_ready")
        s_fhi = sem("ff_hi_ready")
        s_flo = sem("ff_lo_ready")
        s_go = sem("gain_out_landed")
        s_dn = sem("down_psum")
        s_fin = sem("final_ready")
        s_out = sem("out_stored")

        def hb(t, h):
            return t[:, h * S:(h + 1) * S]

        def evacuated(eng, g):
            eng.wait_ge(s_ev[g % 4], g // 4 + 1)

        NORMS = [("in", t) for t in range(TB)] + [("hgrn", 0), ("mix", 0), ("mix", 1), ("ffn", 0)]
        for t in range(2, TB):
            NORMS += [("mix", t), ("ffn", t - 1)]
        NORMS += [("ffn", TB - 1)] + [("out", t) for t in range(TB)]

        def norm(kind, t):
            return NORMS.index((kind, t)) + 1

        def used(eng, j):
            if j < J_WO:
                eng.wait_ge(s_proj, sum(g[0] <= j for g in groups))
            elif j < J_FF:
                eng.wait_ge(*((s_wo, TB) if j == J_FF - 1 else (s_rows, j - J_WO + 1)))
            elif j < J_DN:
                eng.wait_ge(s_gu, 2 * (j - J_FF + 1))
            else:
                eng.wait_ge(s_rows, KT // 2 - 1 + j - J_DN + 1)

        def raw_src(j):
            kind, c = chunks[j]
            if kind == "ikw":
                return wi[:, 8 * W:8 * W + IKW].rearrange("(k p) n -> p k n", p=P)
            if kind in ("wo", "down"):
                src = wo if kind == "wo" else wd
                return src[c * 2 * P:(c + 1) * 2 * P, :].rearrange("(k p) n -> p k n", p=P)
            src = {"gate": wg, "up": wu}.get(kind, wi)
            lo = c * 256 + SEG.get(kind, 0)
            return src[:, lo:lo + 256].rearrange("(k p) n -> p k n", p=P)

        def slot(t, j):
            kind = chunks[j][0]
            if kind == "ikw":
                return t[:, j % 2, 0:KT * IKW].rearrange("p (k n) -> p k n", k=KT)
            return t[:, j % 2, :].rearrange("p (k n) -> p k n", k=2 if kind in ("wo", "down") else KT)

        def upper(t, z, c=None):
            return t.rearrange("p (n u z) -> p n u z", u=2, z=z)

        ctx.enter_context(nc.allow_non_contiguous_dma(reason="lower bounds and group gains go one per partition"))
        block = ctx.enter_context(nc.Block())

        @block.sync
        def _(sp):
            for t in range(TB):
                sp.dma_start(xin[:, t, :], x_d[t * P:(t + 1) * P, :]).then_inc(s_x[t], 16)
                if t == 0:
                    sp.dma_start(gain_in, norm_pre_mix[0, :].partition_broadcast(P)).then_inc(s_gin, 16)
            for j in range(NCH):
                if j >= 2:
                    sp.wait_ge(s_lo, j - 1)
                sp.dma_start(slot(raw, j), raw_src(j)).then_inc(s_raw[j % 2], 16)
            for t in range(TB):
                sp.wait_ge(s_fin, t + 1)
                sp.dma_start(out_d[t * P:(t + 1) * P, :], x2[:, t, :]).then_inc(s_out, 16)
            sp.wait_ge(s_out, 16 * TB)

        @block.gpsimd
        def _(pool):
            n_chain = [0]

            def link(ins):
                n_chain[0] += 1
                ins.then_inc(s_pool, 1)
                pool.wait_ge(s_pool, n_chain[0])

            def inv_root(col, n, width):
                link(pool.tensor_scalar(ms[:, col:col + n], ss[:, col:col + n], 1.0 / width, EPS, ALU.mult, ALU.add))
                pool.tensor_tensor(rstd[:, col:col + n], ms[:, col:col + n], mhalf[:, 0:n], ALU.pow).then_inc(s_rs, 1)

            link(pool.memset(ident[:, :], 0.0))
            pool.affine_select(out=ident[:, :], in_=ident[:, :], compare_op=ALU.not_equal, fill=1.0, base=0,
                               pattern=[[-1, P]], channel_multiplier=1).then_inc(s_const, 1)
            link(pool.memset(mhalf[:, :], -0.5))
            for t in range(TB):
                pool.wait_ge(s_ss, norm("in", t))
                inv_root(t, 1, D)
            link(pool.memset(lmask[:, :, :], 1.0))
            for l, z in enumerate(LEVELS):
                v = lmask[:, l, :].rearrange("p (n z) -> p n z", z=z)
                link(pool.affine_select(out=v, in_=v, compare_op=ALU.is_ge, fill=0.0, base=0,
                                        pattern=[[-2 * z, 64 // z], [0, z]], channel_multiplier=1))
                link(pool.affine_select(out=v, in_=v, compare_op=ALU.is_ge, fill=0.0, base=z - 1,
                                        pattern=[[2 * z, 64 // z], [0, z]], channel_multiplier=-1))
            link(pool.memset(M0[:, :], 0.0))
            pool.affine_select(out=M0[:, :], in_=M0[:, :], compare_op=ALU.is_ge, fill=CLOSED, base=0,
                               pattern=[[-1, P]], channel_multiplier=1).then_inc(s_const, 1)
            pool.wait_ge(s_hx, TB)
            pool.memset(Sd[:, :, :], 0.0).then_inc(s_const, 1)
            pool.wait_ge(s_hps, TB)
            link(pool.memset(Z[1], 1.0))
            pool.memset(Z[1].rearrange("p (n t) -> p n t", t=P)[:, :, 0:1], 0.0).then_inc(s_rst, 1)
            for b in (1, 2, 3):
                pool.wait_ge(s_sc, 8 * b)
                v = SC[b][:, b * P:(b + 1) * P]
                pool.affine_select(out=v, in_=v, compare_op=ALU.is_ge, fill=FUTURE, base=0,
                                   pattern=[[-1, P]], channel_multiplier=1).then_inc(s_fut, 1)
            pool.wait_ge(s_b, 1)
            for l, z in enumerate(LEVELS):
                if l >= 2:
                    pool.wait_ge(s_lvl, 4 * (l - 1))
                b4 = upper(bT, z)
                d4 = upper(Z[l % 2], z)
                edge = b4[:, :, 0, z - 1:z].to_broadcast([P, S * HEADS_A // (2 * z), z])
                pool.tensor_tensor(d4[:, :, 1, :], b4[:, :, 1, :], edge, ALU.subtract)
                pool.tensor_tensor(d4[:, :, 0, :], edge, b4[:, :, 0, :], ALU.subtract).then_inc(s_D, 1)
            pool.wait_ge(s_lvl, 4 * len(LEVELS))
            b3 = bT.rearrange("p (n t) -> p n t", t=P)
            end = b3[:, :, P - 1:P].to_broadcast([P, HEADS_A * TB, P])
            pool.tensor_tensor(Z[0].rearrange("p (n t) -> p n t", t=P), end, b3, ALU.subtract).then_inc(s_D, 1)
            pool.wait_ge(s_gst, 16)
            pool.wait_ge(s_off, len(PAIRS))
            for h in range(HEADS_B):
                pool.dma_start(Bh[:, h, :], bass.AP(tensor=gscr.tensor, offset=h * P * (S + P) + P - 1,
                                                    ap=[[S + P - 1, P], [1, S]])).then_inc(s_bh, 16)
            pool.wait_ge(s_E, len(LEVELS) + 2)
            pool.wait_ge(s_eb, 1)
            for a, gain in enumerate((norm_post_mix, norm_pre_ffn)):
                pool.dma_start(gain_mid[:, a, :], gain[0, :].partition_broadcast(P)).then_inc(s_mid, 16)
            pool.wait_ge(s_lvl, 4 * (len(LEVELS) + 1))
            pool.wait_ge(s_Z, len(LEVELS) + 2)
            for t in range(TB):
                pool.dma_start(x2[:, t, :], x_d[t * P:(t + 1) * P, :]).then_inc(s_mid, 16)
            pool.wait_ge(s_ss, norm("hgrn", 0))
            inv_root(16, 16, DK)
            pool.wait_ge(s_bh, 16 * HEADS_B)
            pool.wait_ge(s_o, TB)
            for u in range(UNITS):
                b, h = divmod(u, HEADS_B)
                n = (b + 1) * P
                if h == 0 and b:
                    pool.wait_ge(s_mask, b)
                if u >= 3:
                    pool.wait_ge(s_nm, u - 2)
                M = M0[:, :] if b == 0 else SC[b]
                pool.tensor_tensor(BM[u % 3][:, 0:n], Bh[:, h, (TB - 1 - b) * P:S], M, ALU.add).then_inc(s_bm, 1)
            for k in range(TB + 1):
                if k < TB:
                    pool.wait_ge(s_ss, norm("mix", k))
                    inv_root(4 + k, 1, D)
                if k >= 1:
                    pool.wait_ge(s_ss, norm("ffn", k - 1))
                    inv_root(8 + k - 1, 1, D)
            pool.wait_ge(s_bm, UNITS)
            pool.dma_start(gain_out, norm_post_ffn[0, :].partition_broadcast(P)).then_inc(s_go, 16)
            for t in range(TB):
                pool.wait_ge(s_ss, norm("out", t))
                inv_root(12 + t, 1, D)

        @block.scalar
        def _(act):
            def split(j):
                act.wait_ge(s_raw[j % 2], 16 * (j // 2 + 1))
                if j >= 2:
                    used(act, j - 2)
                act.activation(slot(w_hi, j), slot(raw, j), ACT.Copy).then_inc(s_hi, 1)

            def turn_hi(n, banks, t):
                act.wait_ge(s_hps, n + 1)
                act.activation(hT_hi[:, :, t * P:(t + 1) * P],
                               PS[:, banks:banks + 2, :].rearrange("p a (k t) -> p (a k) t", t=P),
                               ACT.Copy).then_inc(s_hhi, 1)

            act.dma_start(lbt[:, :, :], lb_logits.rearrange("r (h p) -> p r h", p=P)).then_inc(s_small, 16)
            act.dma_start(gn[:, :], hgrn_gnorm.rearrange("a p -> p a")).then_inc(s_small, 16)
            act.dma_start(tab, rel_bias).then_inc(s_small, 16)
            act.dma_start(oh_sb, onehot).then_inc(s_small, 16)
            for t in range(TB):
                act.wait_ge(s_x[t], 16)
                act.wait_ge(s_ss, t) if t else None
                act.activation(scr[0], xin[:, t, :], ACT.Square, accum_out=ss[:, t:t + 1]).then_inc(s_ss, 1)
            act.wait_ge(s_lbm, 1)
            act.activation(lbw[:, 1:3, :], lbt[:, :, :], ACT.Exp).then_inc(s_lbe, 1)
            for t in range(TB):
                turn_hi(t, 2 * (t % 2), t)
                if t == 1:
                    split(0)
            act.wait_ge(s_gps, 1)
            act.activation(g_sb[:, 0:S], PS[0:HEADS_B, 4, :], ACT.Copy)
            act.activation(g_sb[:, S:S + P], PS[0:HEADS_B, 5, 0:P], ACT.Copy).then_inc(s_gsb, 1)
            act.wait_ge(s_gsb, 1)
            act.dma_start(gscr, g_sb.unsqueeze(1).to_broadcast([HEADS_B, P, S + P])).then_inc(s_gst, 16)

            def evac(g):
                j, kind, c, m = groups[g]
                if kind in ("f", "q", "g", "iq", "ikw", "aq", "ak", "i", "av"):
                    act.wait_ge(s_proj, g + 1)
                ps = PS[:, g % 4, :]
                done = s_ev[g % 4]
                h = 2 * c + m
                if kind == "iq":
                    act.activation(hb(iqT, h), ps, ACT.Copy).then_inc(done, 1)
                elif kind == "ikw":
                    act.activation(ikT[0:DH, :], ps[0:DH, :], ACT.Copy)
                    act.activation(ikT[DH:P, :], ps[0:DH, :], ACT.Copy)
                    act.activation(iwT[DH:IKW, :], ps[DH:IKW, :], ACT.Copy).then_inc(done, 1)
                elif kind == "f":
                    act.wait_ge(s_gst, 16)
                    act.activation(hb(kT, h), ps, ACT.Sigmoid).then_inc(done, 1)
                elif kind in ("q", "g"):
                    act.activation(hb(qT if kind == "q" else gT, h), ps, ACT.Sigmoid).then_inc(s_sig, 1)
                elif kind in ("i", "av"):
                    dst = (V if kind == "i" else av).rearrange("p (t n) -> p t n", t=TB)
                    if kind == "av" and c == 0 and m == 0:
                        act.wait_ge(s_dot, 24)
                    act.activation(dst[:, 2 * m:2 * m + 2, c * 256:(c + 1) * 256],
                                   ps.rearrange("p (t n) -> p t n", t=2), ACT.Copy).then_inc(done, 1)
                elif kind == "aq":
                    act.wait_ge(s_dot, 24)
                    act.activation(hb(aqT, h), ps, ACT.Copy, scale=DH ** -0.5).then_inc(done, 1)
                else:
                    act.activation(hb(akT, h), ps, ACT.Copy).then_inc(done, 1)

            g = 0
            for j in range(J_WO):
                split(j + 1)
                while g < len(groups) and groups[g][0] == j:
                    evac(g)
                    g += 1
                if j == 2:
                    for u in range(24):
                        n = (u // 8 + 2) * P
                        act.wait_ge(s_dot, u + 1)
                        if u >= 2:
                            act.wait_ge(s_sc, u - 1)
                        act.activation(rl[u % 2][:, 0:n], PS[:, 4 + u % 2, 0:n], ACT.Relu).then_inc(s_rl, 1)
                if j == 4:
                    act.wait_ge(s_f, 1)
                    act.activation(Z[0], bT, ACT.Ln).then_inc(s_ln, 1)
                if J_LEVEL - 1 <= j < J_LEVEL - 1 + len(LEVELS):
                    l = j - (J_LEVEL - 1)
                    act.wait_ge(s_D, l + 1)
                    act.activation(Z[l % 2], Z[l % 2], ACT.Exp).then_inc(s_E, 1)
                if j == J_LEVEL + len(LEVELS) - 1:
                    b4 = bT.rearrange("p (h c t) -> p h c t", h=HEADS_A, c=TB)
                    act.activation(eB[:, :, :], b4[:, :, :, P - 1], ACT.Exp).then_inc(s_eb, 1)
                    act.wait_ge(s_lvl, 4 * (len(LEVELS) - 1))
                    act.wait_ge(s_D, len(LEVELS))
                    act.activation(Z[1], bT, ACT.Exp).then_inc(s_E, 1)
                    act.wait_ge(s_D, len(LEVELS) + 1)
                    act.activation(Z[0], Z[0], ACT.Exp).then_inc(s_E, 1)
                if j == J_LEVEL + len(LEVELS) + 1:
                    for i in range(len(PAIRS)):
                        act.wait_ge(s_off, i + 1)
                        act.activation(So[:, i, :], PS[:, 4 + i % 4, :], ACT.Copy).then_inc(s_ofs, 1)
            split(J_WO + 1)
            act.wait_ge(s_ya, TB)
            for i in range(16):
                if i == 8:
                    o.then_inc(s_half, 1)
                    act.wait_ge(s_half, 1)
                o = act.activation(scr[0][:, i % 8 * DK:(i % 8 + 1) * DK], ya[:, i * DK:(i + 1) * DK], ACT.Square,
                                   accum_out=ss[:, 16 + i:17 + i])
            o.then_inc(s_ss, 1)

            def y_hi_a():
                act.wait_ge(s_yg, TB)
                used(act, J_WO - 1)
                act.activation(hT_hi[:, 0:4, :], gT.rearrange("p (h t) -> p h t", t=S), ACT.Copy).then_inc(s_yhi, 1)

            def y_hi_b(b):
                act.wait_ge(s_pv, 8 * b + 8)
                act.activation(hT_hi[:, 4:8, b * P:(b + 1) * P],
                               PS[:, 4 + b, :].rearrange("p (k t) -> p k t", t=P), ACT.Copy).then_inc(s_yhi, 1)

            for i in range(UNITS + 3):
                if i < UNITS:
                    n = (i // 8 + 1) * P
                    act.wait_ge(s_nm, i + 1)
                    act.activation(Pb[i % 3][:, 0:n], Pb[i % 3][:, 0:n], ACT.Exp, bias=nm[:, i:i + 1],
                                   accum_out=sm[:, i:i + 1]).then_inc(s_ex, 1)
                if 2 <= i < UNITS + 2:
                    u = i - 2
                    n = (u // 8 + 1) * P
                    act.wait_ge(s_ptp, u + 1)
                    if u >= 2:
                        act.wait_ge(s_pv, u - 1)
                    act.activation(PT[u % 2][:, 0:n], PS[:, 2 + u % 2, 0:n], ACT.Copy).then_inc(s_pts, 1)
                if i == 6:
                    y_hi_a()
                if i >= 11 and (i - 11) % 8 == 0 and (i - 11) // 8 < TB - 1:
                    y_hi_b((i - 11) // 8)
            y_hi_b(TB - 1)
            split(J_WO + 2)
            split(J_WO + 3)
            split(J_WO + 4)
            for k in range(TB + 2):
                if k < TB:
                    act.wait_ge(s_wo, k + 1)
                    act.wait_ge(s_ss, norm("mix", k) - 1)
                    act.activation(junk, PS[:, 2 * k:2 * k + 2, :].rearrange("p a n -> p (a n)"),
                                   ACT.Square, accum_out=ss[:, 4 + k:5 + k]).then_inc(s_ss, 1)
                if 1 <= k <= TB:
                    act.wait_ge(s_x2, k)
                    act.wait_ge(s_ss, norm("ffn", k - 1) - 1)
                    act.activation(junk, x2[:, k - 1, :], ACT.Square, accum_out=ss[:, 7 + k:8 + k]).then_inc(s_ss, 1)
                if k >= 2:
                    turn_hi(TB + k - 2, 2 * (k - 2), k - 2)
            split(J_FF + 1)
            for i in range(FT // 2):
                split(J_FF + 2 * i + 2)
                for f in (2 * i, 2 * i + 1):
                    act.wait_ge(s_gu, 2 * (f // 2) * 2 + (f % 2) + 1)
                    if f >= 2:
                        act.wait_ge(s_fr, f - 1)
                    act.activation(sig[f % 2], PS[:, f % 2, :], ACT.Sigmoid).then_inc(s_fs, 1)
                act.wait_ge(s_fr, 2 * i + 1)
                act.activation(ff[:, 2 * i, 0, :], fraw[0], ACT.Copy).then_inc(s_fhi, 1)
                split(J_FF + 2 * i + 3)
                act.wait_ge(s_fr, 2 * i + 2)
                act.activation(ff[:, 2 * i + 1, 0, :], fraw[1], ACT.Copy).then_inc(s_fhi, 1)
            for j in range(J_DN + 2, NCH):
                split(j)
            for t in range(TB):
                act.wait_ge(s_dn, t + 1)
                act.wait_ge(s_ss, norm("out", t) - 1)
                act.activation(raw[:, t % 2, 0:D], PS[:, 2 * t:2 * t + 2, :].rearrange("p a n -> p (a n)"),
                               ACT.Square, accum_out=ss[:, 12 + t:13 + t]).then_inc(s_ss, 1)

        @block.vector
        def _(dve):
            n_chain = [0]

            def link(ins):
                n_chain[0] += 1
                ins.then_inc(s_dve, 1)
                dve.wait_ge(s_dve, n_chain[0])

            def split(j):
                dve.wait_ge(s_hi, j + 1)
                dve.tensor_tensor(slot(w_lo, j), slot(raw, j), slot(w_hi, j).bitcast(F32),
                                  ALU.subtract).then_inc(s_lo, 1)

            def turn_lo(n, banks, t):
                dve.wait_ge(s_hhi, n + 1)
                dve.tensor_tensor(hT_lo[:, :, t * P:(t + 1) * P],
                                  PS[:, banks:banks + 2, :].rearrange("p a (k t) -> p (a k) t", t=P),
                                  hT_hi[:, :, t * P:(t + 1) * P].bitcast(F32), ALU.subtract).then_inc(s_hlo, 1)

            dve.wait_ge(s_small, 64)
            link(dve.tensor_tensor(lbw[:, 0, :], lbt[:, 0, :], lbt[:, 1, :], ALU.max))
            for r in range(2):
                o = dve.tensor_tensor(lbt[:, r, :], lbt[:, r, :], lbw[:, 0, :], ALU.subtract)
            o.then_inc(s_lbm, 1)
            dve.wait_ge(s_gin, 16)
            for t in range(TB):
                dve.wait_ge(s_rs, norm("in", t))
                dve.scalar_tensor_tensor(out=xin[:, t, :], in0=xin[:, t, :], scalar=rstd[:, t:t + 1], in1=gain_in,
                                         op0=ALU.mult, op1=ALU.mult).then_inc(s_hx, 1)
                if t >= 1:
                    turn_lo(t - 1, 2 * ((t - 1) % 2), t - 1)
            turn_lo(TB - 1, 2 * ((TB - 1) % 2), TB - 1)
            split(0)
            dve.wait_ge(s_lbe, 1)
            link(dve.tensor_tensor(lbw[:, 3, :], lbw[:, 1, :], lbw[:, 2, :], ALU.add))
            link(dve.reciprocal(lbw[:, 3, :], lbw[:, 3, :]))
            link(dve.tensor_tensor(lbw[:, 4, :], lbw[:, 1, :], lbw[:, 3, :], ALU.mult))
            link(dve.tensor_scalar(lbw[:, 5, :], lbw[:, 4, :], -1.0, 1.0, ALU.mult, ALU.add))

            def silu_mul(g):
                j, kind, c, m = groups[g]
                n_sig = g - first_group["q"] if kind == "q" else g - first_group["g"] + 4
                dve.wait_ge(s_sig, n_sig + 1)
                dst = hb(qT if kind == "q" else gT, 2 * c + m)
                dve.tensor_tensor(dst, PS[:, g % 4, :], dst, ALU.mult).then_inc(s_ev[g % 4], 1)

            def topk_round(r):
                b, k = r // 16 + 1, r % 16
                if k == 0:
                    dve.wait_ge(s_fut, b)
                link(dve.max(top8[:, :], SC[b]))
                link(dve.match_replace(SC[b], top8[:, :], SC[b], TAKEN))
                if k == 15:
                    dve.tensor_scalar(SC[b], SC[b], 0.5 * (FUTURE + TAKEN), CLOSED, ALU.is_gt,
                                      ALU.mult).then_inc(s_mask, 1)

            rounds = iter(range(48))

            def topk_rounds(n):
                for _, r in zip(range(n), rounds):
                    topk_round(r)

            def merge(l):
                z = LEVELS[l]
                if l:
                    dve.wait_ge(s_ma, 4 * l)
                for c in range(TB):
                    dve.wait_ge(s_lvl, 4 * l + c + 1)
                    v = Sd[:, c, :].rearrange("p (h n u z) -> p h n u z", h=HEADS_A, u=2, z=z)[:, :, :, 1, :]
                    s = PS[:, 4 + c, :].rearrange("p (h n u z) -> p h n u z", h=HEADS_A, u=2, z=z)[:, :, :, 1, :]
                    m = lmask[:, l, :].rearrange("p (n z) -> p n z", z=z).bitcast(U32)
                    for h in range(HEADS_A):
                        o = dve.copy_predicated(v[:, h], m, s[:, h])
                    o.then_inc(s_ma, 1)

            def chunk_ends():
                dve.wait_ge(s_E, len(LEVELS) + 1)
                link(dve.tensor_tensor(Z[1], Z[1], qT, ALU.mult))
                dve.wait_ge(s_E, len(LEVELS) + 2)
                link(dve.tensor_tensor(Z[0], Z[0], kT, ALU.mult))
                dve.wait_ge(s_eb, 1)
                for h in range(HEADS_A):
                    dve.tensor_scalar(UX[:, h * P:(h + 1) * P], hb(Z[1], h)[:, 3 * P:4 * P], eB[:, h, 2:3], None,
                                      ALU.mult)
                    o = dve.tensor_scalar(LX[:, h * P:(h + 1) * P], hb(Z[0], h)[:, 0:P], eB[:, h, 1:2], None,
                                          ALU.mult)
                o.then_inc(s_Z, 2)

            def diagonal():
                dve.wait_ge(s_ma, 4 * len(LEVELS))
                for c in range(TB):
                    dve.wait_ge(s_lvl, 4 * len(LEVELS) + c + 1)
                    for h in range(HEADS_A):
                        o = dve.copy_predicated(Sd[:, c, h * P:(h + 1) * P], ident[:, :].bitcast(U32),
                                                PS[:, 4 + c, h * P:(h + 1) * P])
                    o.then_inc(s_ma, 1)

            for j in range(J_WO):
                split(j + 1)
                for g in range(len(groups)):
                    if groups[g][0] == j and groups[g][1] in ("q", "g"):
                        silu_mul(g)
                if j == 2:
                    dve.wait_ge(s_iwp, 1)
                    dve.tensor_scalar(iw[:, :, :], PS[:, 6, 0:TB * HEADS_B].rearrange("p (t h) -> p t h", t=TB),
                                      HEADS_B ** -0.5 * DH ** -0.5, None, ALU.mult).then_inc(s_iws, 1)
                    dve.wait_ge(s_iws, 1)
                    for u in range(24):
                        b, h = u // 8 + 1, u % 8
                        n = (b + 1) * P
                        dve.wait_ge(s_rl, u + 1)
                        if h == 0:
                            o = dve.tensor_scalar(SC[b], rl[u % 2][:, 0:n], iw[:, b, h:h + 1], None, ALU.mult)
                        else:
                            dve.wait_ge(s_sc, u)
                            o = dve.scalar_tensor_tensor(out=SC[b], in0=rl[u % 2][:, 0:n], scalar=iw[:, b, h:h + 1],
                                                         in1=SC[b], op0=ALU.mult, op1=ALU.add)
                        o.then_inc(s_sc, 1)
                elif j == 4:
                    for h in range(HEADS_A):
                        evacuated(dve, first_group["f"] + h)
                        o = dve.tensor_scalar(hb(bT, h), hb(kT, h), lbw[:, 5, h:h + 1], lbw[:, 4, h:h + 1],
                                              ALU.mult, ALU.add)
                    link(o)
                    dve.tensor_scalar(kT, bT, -1.0, 1.0, ALU.mult, ALU.add).then_inc(s_f, 1)
                elif j == 5:
                    dve.wait_ge(s_ln, 1)
                    dve.wait_ge(s_rst, 1)
                    dve.tensor_tensor_scan(bT, Z[1], Z[0], 0.0, ALU.mult, ALU.add).then_inc(s_b, 1)
                if J_LEVEL - 1 <= j < J_LEVEL - 1 + len(LEVELS):
                    l = j - (J_LEVEL - 1)
                    z = LEVELS[l]
                    dve.wait_ge(s_E, l + 1)
                    if l == 0:
                        for h in range(HEADS_A):
                            evacuated(dve, first_group["q"] + h)
                    z4 = upper(Z[l % 2], z)
                    dve.tensor_tensor(z4[:, :, 1, :], z4[:, :, 1, :], upper(qT, z)[:, :, 1, :], ALU.mult)
                    dve.tensor_tensor(z4[:, :, 0, :], z4[:, :, 0, :], upper(kT, z)[:, :, 0, :],
                                      ALU.mult).then_inc(s_Z, 1)
                if j >= J_LEVEL and j - J_LEVEL < len(LEVELS):
                    if j == J_LEVEL:
                        dve.wait_ge(s_const, 3)
                    merge(j - J_LEVEL)
                if j == J_LEVEL + len(LEVELS):
                    chunk_ends()
                    diagonal()
                if j >= 3:
                    topk_rounds(4)
            for c in range(TB):
                dve.wait_ge(s_o, c + 1)
                dve.tensor_copy(ya[:, c * W:(c + 1) * W], PS[:, 4 + c, :]).then_inc(s_ya, 1)
            split(J_WO + 1)

            def y_norm():
                dve.wait_ge(s_rs, norm("hgrn", 0))
                v = ya.rearrange("p (n d) -> p n d", d=DK)
                dve.tensor_tensor(v, v, rstd[:, 16:32].unsqueeze(2).to_broadcast([P, 16, DK]),
                                  ALU.mult).then_inc(s_yn, 1)

            def y_gate():
                for h in range(HEADS_A):
                    evacuated(dve, first_group["g"] + h)
                for t in range(TB):
                    dve.wait_ge(s_yt, t + 1)
                    v = gT.rearrange("p (h t) -> p h t", t=S)[:, :, t * P:(t + 1) * P]
                    dve.scalar_tensor_tensor(out=v, in0=PS[:, 6 + t % 2, :].rearrange("p (h t) -> p h t", t=P),
                                             scalar=gn[:, 0:1], in1=v, op0=ALU.mult, op1=ALU.mult).then_inc(s_yg, 1)

            def y_lo_a():
                dve.wait_ge(s_yhi, 1)
                dve.tensor_tensor(hT_lo[:, 0:4, :], gT.rearrange("p (h t) -> p h t", t=S),
                                  hT_hi[:, 0:4, :].bitcast(F32), ALU.subtract).then_inc(s_ylo, 1)

            def y_lo_b(b):
                dve.wait_ge(s_yhi, b + 2)
                dve.tensor_tensor(hT_lo[:, 4:8, b * P:(b + 1) * P], PS[:, 4 + b, :].rearrange("p (k t) -> p k t", t=P),
                                  hT_hi[:, 4:8, b * P:(b + 1) * P].bitcast(F32), ALU.subtract).then_inc(s_ylo, 1)

            for i in range(UNITS + 3):
                if i < UNITS:
                    n = (i // 8 + 1) * P
                    dve.wait_ge(s_qk, i + 1)
                    dve.wait_ge(s_bm, i + 1)
                    if i >= 3:
                        dve.wait_ge(s_ptp, i - 2)
                    link(dve.tensor_tensor_reduce(Pb[i % 3][:, 0:n], PS[:, i % 2, 0:n], BM[i % 3][:, 0:n], 1.0,
                                                  -3.4e38, ALU.add, ALU.max, mx[:, i:i + 1]))
                    dve.tensor_scalar(nm[:, i:i + 1], mx[:, i:i + 1], -1.0, None, ALU.mult).then_inc(s_nm, 1)
                if 1 <= i <= UNITS:
                    u = i - 1
                    n = (u // 8 + 1) * P
                    dve.wait_ge(s_ex, u + 1)
                    link(dve.reciprocal(rs[:, u:u + 1], sm[:, u:u + 1]))
                    dve.tensor_scalar(Pb[u % 3][:, 0:n], Pb[u % 3][:, 0:n], rs[:, u:u + 1], None,
                                      ALU.mult).then_inc(s_pn, 1)
                if i == 1:
                    y_norm()
                if i == 3:
                    y_gate()
                if i == 7:
                    y_lo_a()
                if i >= 11 and (i - 11) % 8 == 0 and (i - 11) // 8 < TB - 1:
                    y_lo_b((i - 11) // 8)
            y_lo_b(TB - 1)
            split(J_WO + 2)
            split(J_WO + 3)
            split(J_WO + 4)
            dve.wait_ge(s_mid, 16 * 6)
            for k in range(TB + 2):
                if k < TB:
                    dve.wait_ge(s_rs, norm("mix", k))
                    if k >= 2:
                        dve.wait_ge(s_hps, TB + k - 1)
                    o = dve.scalar_tensor_tensor(out=scr[k % 2], in0=PS[:, 2 * k:2 * k + 2, :].rearrange("p a n -> p (a n)"),
                                                 scalar=rstd[:, 4 + k:5 + k], in1=gain_mid[:, 0, :],
                                                 op0=ALU.mult, op1=ALU.mult)
                    o.then_inc(s_pa, 1)
                    dve.wait_ge(s_pa, k + 1)
                    dve.tensor_tensor(x2[:, k, :], x2[:, k, :], scr[k % 2], ALU.add).then_inc(s_x2, 1)
                if 1 <= k <= TB:
                    dve.wait_ge(s_rs, norm("ffn", k - 1))
                    dve.wait_ge(s_x2, k)
                    dve.scalar_tensor_tensor(out=scr[(k - 1) % 2], in0=x2[:, k - 1, :], scalar=rstd[:, 7 + k:8 + k],
                                             in1=gain_mid[:, 1, :], op0=ALU.mult, op1=ALU.mult).then_inc(s_hx, 1)
                if k >= 2:
                    turn_lo(TB + k - 2, 2 * (k - 2), k - 2)
            split(J_FF + 1)

            def ff_mul(f):
                dve.wait_ge(s_fs, f + 1)
                link(dve.tensor_tensor(sig[f % 2], PS[:, f % 2, :], sig[f % 2], ALU.mult))
                dve.wait_ge(s_gu, 4 * (f // 2) + 2 + f % 2 + 1)
                if f >= 2:
                    dve.wait_ge(s_fhi, f - 1)
                dve.tensor_tensor(fraw[f % 2], PS[:, 2 + f % 2, :], sig[f % 2], ALU.mult).then_inc(s_fr, 1)

            def ff_lo(f):
                dve.wait_ge(s_fhi, f + 1)
                dve.tensor_tensor(ff[:, f, 1, :], fraw[f % 2], ff[:, f, 0, :].bitcast(F32),
                                  ALU.subtract).then_inc(s_flo, 1)

            for i in range(FT // 2):
                split(J_FF + 2 * i + 2)
                ff_mul(2 * i)
                ff_lo(2 * i)
                split(J_FF + 2 * i + 3)
                ff_mul(2 * i + 1)
                ff_lo(2 * i + 1)
            for j in range(J_DN + 2, NCH):
                split(j)
            dve.wait_ge(s_go, 16)
            for t in range(TB):
                dve.wait_ge(s_rs, norm("out", t))
                o = raw[:, t % 2, D:2 * D]
                link(dve.scalar_tensor_tensor(out=o, in0=PS[:, 2 * t:2 * t + 2, :].rearrange("p a n -> p (a n)"),
                                              scalar=rstd[:, 12 + t:13 + t], in1=gain_out,
                                              op0=ALU.mult, op1=ALU.mult))
                dve.tensor_tensor(x2[:, t, :], x2[:, t, :], o, ALU.add).then_inc(s_fin, 1)

        @block.tensor
        def _(pe):
            def passes(k, lhs, rhs, out, first, last):
                for n, (a, b) in enumerate(((0, 1), (1, 0), (0, 0))):
                    o = pe.matmul(out, lhs[a], rhs[b], start=(first and n == 0), stop=(last and n == 2))
                return o

            def weights(j):
                return slot(w_hi, j), slot(w_lo, j)

            def project(j):
                pe.wait_ge(s_lo, j + 1)
                w = weights(j)
                for g in range(len(groups)):
                    if groups[g][0] != j:
                        continue
                    kind, m = groups[g][1], groups[g][3]
                    if g >= 4:
                        evacuated(pe, g - 4)
                    if kind in ("i", "av"):
                        for tt in range(2):
                            t = 2 * m + tt
                            for k in range(KT):
                                o = passes(k, [hT[:, k, t * P:(t + 1) * P] for hT in (hT_hi, hT_lo)],
                                           [x[:, k, :] for x in w], PS[:, g % 4, tt * 256:(tt + 1) * 256],
                                           k == 0, k == KT - 1)
                    else:
                        M = IKW if kind == "ikw" else P
                        for k in range(KT):
                            o = passes(k, [x[:, k, m * M:(m + 1) * M] for x in w],
                                       [hT[:, k, :] for hT in (hT_hi, hT_lo)], PS[0:M, g % 4, :],
                                       k == 0, k == KT - 1)
                    o.then_inc(s_proj, 1)

            def turn(src, bank):
                for k in range(KT):
                    o = pe.transpose(PS[:, bank + k // 4, (k % 4) * P:(k % 4 + 1) * P],
                                     src[:, k * P:(k + 1) * P], ident[:, :])
                o.then_inc(s_hps, 1)

            def indexer_dots():
                evacuated(pe, first_group["ikw"])
                for t in range(TB):
                    o = pe.transpose(PS[:, 6, t * HEADS_B:(t + 1) * HEADS_B], iwT[DH:IKW, t * P:(t + 1) * P],
                                     ident[DH:IKW, DH:IKW])
                o.then_inc(s_iwp, 1)
                for g in range(4):
                    evacuated(pe, first_group["iq"] + g)
                for u in range(24):
                    b, h = u // 8 + 1, u % 8
                    r = (h % 2) * DH
                    if u >= 2:
                        pe.wait_ge(s_rl, u - 1)
                    pe.matmul(PS[:, 4 + u % 2, 0:(b + 1) * P], hb(iqT, h // 2)[r:r + DH, b * P:(b + 1) * P],
                              ikT[r:r + DH, 0:(b + 1) * P], start=True, stop=True).then_inc(s_dot, 1)

            def level(l):
                if l < len(LEVELS):
                    pe.wait_ge(s_Z, l + 1)
                if l == 0:
                    pe.wait_ge(s_iws, 1)
                for c in range(TB):
                    if l >= 1:
                        pe.wait_ge(s_ma, 4 * (l - 1) + c + 1)
                    for h in range(HEADS_A):
                        a = hb(Z[l % 2] if l < len(LEVELS) else kT, h)[:, c * P:(c + 1) * P]
                        b = hb(Z[l % 2] if l < len(LEVELS) else qT, h)[:, c * P:(c + 1) * P]
                        o = pe.matmul(PS[:, 4 + c, h * P:(h + 1) * P], a, b, start=True, stop=True)
                    o.then_inc(s_lvl, 1)

            def between_chunks():
                pe.wait_ge(s_Z, len(LEVELS) + 2)
                for i, (c, s) in enumerate(PAIRS):
                    if i < 4:
                        pe.wait_ge(s_ma, 4 * len(LEVELS) + i + 1)
                    else:
                        pe.wait_ge(s_ofs, i - 3)
                    for h in range(HEADS_A):
                        q = UX[:, h * P:(h + 1) * P] if c == 3 and s < 2 else hb(Z[1], h)[:, c * P:(c + 1) * P]
                        k = LX[:, h * P:(h + 1) * P] if c > 1 and s == 0 else hb(Z[0], h)[:, s * P:(s + 1) * P]
                        o = pe.matmul(PS[:, 4 + i % 4, h * P:(h + 1) * P], k, q, start=True, stop=True)
                    o.then_inc(s_off, 1)

            def recurrence_out():
                pe.wait_ge(s_ofs, len(PAIRS))
                pe.wait_ge(s_ma, 4 * (len(LEVELS) + 1))
                for g in range(4):
                    evacuated(pe, first_group["i"] + g)
                for c in range(TB):
                    for h in range(HEADS_A):
                        for s in range(c + 1):
                            S_t = Sd[:, c, :] if s == c else So[:, PAIRS.index((c, s)), :]
                            o = pe.matmul(PS[:, 4 + c, h * P:(h + 1) * P], S_t[:, h * P:(h + 1) * P],
                                          V[:, s * W + h * DK:s * W + (h + 1) * DK], start=(s == 0), stop=(s == c))
                    o.then_inc(s_o, 1)

            pe.wait_ge(s_small, 64)
            pe.matmul(PS[0:HEADS_B, 4, :], tab, oh_sb[:, 0:S], start=True, stop=True)
            pe.matmul(PS[0:HEADS_B, 5, 0:P], tab, oh_sb[:, S:S + P], start=True, stop=True).then_inc(s_gps, 1)
            pe.wait_ge(s_const, 1)
            for t in range(TB):
                pe.wait_ge(s_hx, t + 1)
                if t >= 2:
                    pe.wait_ge(s_hlo, t - 1)
                turn(xin[:, t, :], 2 * (t % 2))
            pe.wait_ge(s_hlo, TB)
            pe.wait_ge(s_gsb, 1)
            for j in range(J_WO):
                project(j)
                if j == 2:
                    indexer_dots()
                if J_LEVEL <= j <= J_LEVEL + len(LEVELS):
                    level(j - J_LEVEL)
                if j == J_LEVEL + len(LEVELS) + 1:
                    between_chunks()
            recurrence_out()

            for g in range(first_group["aq"], len(groups)):
                evacuated(pe, g)
            for i in range(UNITS + 3):
                if i < UNITS:
                    b, h = divmod(i, HEADS_B)
                    r = (h % 2) * DH
                    if i >= 2:
                        pe.wait_ge(s_nm, i - 1)
                    pe.matmul(PS[:, i % 2, 0:(b + 1) * P], hb(aqT, h // 2)[r:r + DH, b * P:(b + 1) * P],
                              hb(akT, h // 2)[r:r + DH, 0:(b + 1) * P], start=True, stop=True).then_inc(s_qk, 1)
                if 2 <= i < UNITS + 2:
                    u = i - 2
                    pe.wait_ge(s_pn, u + 1)
                    if u >= 2:
                        pe.wait_ge(s_pts, u - 1)
                    for s in range(u // HEADS_B + 1):
                        o = pe.transpose(PS[:, 2 + u % 2, s * P:(s + 1) * P], Pb[u % 3][:, s * P:(s + 1) * P],
                                         ident[:, :])
                    o.then_inc(s_ptp, 1)
                if i >= 3:
                    u = i - 3
                    b, h = divmod(u, HEADS_B)
                    r = (h % 2) * DH
                    pe.wait_ge(s_pts, u + 1)
                    if b == 2 and h == 0:
                        pe.wait_ge(s_yg, TB)
                    if b == 0 and h == 0:
                        pe.wait_ge(s_ya, TB)
                    for s in range(b + 1):
                        o = pe.matmul(PS[r:r + DH, 4 + b, (h // 2) * P:(h // 2 + 1) * P],
                                      av[:, s * W + h * DH:s * W + (h + 1) * DH], PT[u % 2][:, s * P:(s + 1) * P],
                                      start=(s == 0), stop=(s == b))
                    o.then_inc(s_pv, 1)
                if i == 3:
                    pe.wait_ge(s_yn, 1)
                    for t in range(TB):
                        if t >= 2:
                            pe.wait_ge(s_yg, t - 1)
                        for h in range(HEADS_A):
                            o = pe.transpose(PS[:, 6 + t % 2, h * P:(h + 1) * P],
                                             ya[:, t * W + h * DK:t * W + (h + 1) * DK], ident[:, :])
                        o.then_inc(s_yt, 1)

            def rows(j, k0, acts, order, first, last, done):
                w = weights(j)
                for t in order:
                    for kk in range(2):
                        k = k0 + kk
                        for half in range(2):
                            o = passes(k, [x[:, t * P:(t + 1) * P] for x in acts(k)],
                                       [x[:, kk, half * 512:(half + 1) * 512] for x in w],
                                       PS[:, 2 * t + half, :], first and kk == 0, last and kk == 1)
                    if last:
                        o.then_inc(done, 1)
                if not last:
                    o.then_inc(s_rows, 1)

            pe.wait_ge(s_ylo, TB + 1)
            for c in range(KT // 2):
                pe.wait_ge(s_lo, J_WO + c + 1)
                rows(J_WO + c, 2 * c, lambda k: (hT_hi[:, k, :], hT_lo[:, k, :]), range(TB), c == 0,
                     c == KT // 2 - 1, s_wo)
            for t in range(TB):
                pe.wait_ge(s_hx, TB + t + 1)
                turn(scr[t % 2], 2 * t)
            pe.wait_ge(s_hlo, 2 * TB)
            for j in range(J_FF, J_DN):
                c, up = divmod(j - J_FF, 2)
                pe.wait_ge(s_lo, j + 1)
                w = weights(j)
                for m in range(2):
                    if c >= 1:
                        pe.wait_ge(s_fr, 2 * (c - 1) + m + 1)
                    for k in range(KT):
                        o = passes(k, [x[:, k, m * P:(m + 1) * P] for x in w],
                                   [hT[:, k, :] for hT in (hT_hi, hT_lo)], PS[:, 2 * up + m, :],
                                   k == 0, k == KT - 1)
                    o.then_inc(s_gu, 1)
            for c in range(FT // 2):
                pe.wait_ge(s_lo, J_DN + c + 1)
                if c == 0:
                    pe.wait_ge(s_fr, FT)
                pe.wait_ge(s_flo, 2 * c + 2)
                rows(J_DN + c, 2 * c, lambda k: (ff[:, k, 0, :], ff[:, k, 1, :]), range(TB), c == 0,
                     c == FT // 2 - 1, s_dn)

    return nc


_INS = ['x', 'w_in', 'lb_logits', 'hgrn_gnorm', 'rel_bias', 'w_o', 'norm_pre_mix', 'norm_post_mix',
        'norm_pre_ffn', 'norm_post_ffn', 'w_gate', 'w_up', 'w_down']
_OUTS = [((1, 512, 1024), 'float32')]


def kernel(**inputs):
    import numpy as _np
    import concourse.bacc as _bacc
    from concourse import mybir as _mybir
    from concourse.bass_utils import run_bass_kernel_spmd as _run

    nc = _bacc.Bacc("TRN2", target_bir_lowering=False, num_devices=1)
    arrays, args = {}, []
    for name in _INS:
        a = _np.ascontiguousarray(inputs[name])
        arrays[f"in_{name}_dram"] = a
        args.append(nc.dram_tensor(f"in_{name}_dram", a.shape, _mybir.dt.from_np(a.dtype), kind="ExternalInput").ap())
    onehot = bucket_onehot(inputs["x"].shape[1])
    arrays["onehot_dram"] = onehot
    args.append(nc.dram_tensor("onehot_dram", onehot.shape, _mybir.dt.from_np(onehot.dtype),
                               kind="ExternalInput").ap())
    for i, (shape, dtype) in enumerate(_OUTS):
        dt = _mybir.dt.from_np(_np.dtype(dtype))
        args.append(nc.dram_tensor(f"out_{i}_dram", shape, dt, kind="ExternalOutput").ap())
    hymba_layer(nc, *args)
    r = _run(nc, [arrays], core_ids=[0])
    got = tuple(r.results[0][f"out_{i}_dram"] for i in range(len(_OUTS)))
    return got[0]
```

```python
from contextlib import ExitStack

import numpy as np

import concourse.bass as bass
from concourse import mybir

P = 128
F32 = mybir.dt.float32
F32R = mybir.dt.float32r
U32 = mybir.dt.uint32
ALU = mybir.AluOpType
ACT = mybir.ActivationFunctionType
AX = mybir.AxisListType

HEADS_A, DK = 4, 128
HEADS_B, DH = 8, 64
TOPK_MAX = 256
N_BUCKETS, MAX_DISTANCE = 32, 128
EPS = 1e-6
FUTURE = -2.0e38
TAKEN = -3.0e38
CLOSED = -1.0e30


def bucket_onehot(seq):
    exact = N_BUCKETS // 2
    n = np.maximum(seq - 1 - np.arange(seq + P), 0)
    large = exact + (np.log(np.maximum(n, 1) / exact) / np.log(MAX_DISTANCE / exact)
                     * (N_BUCKETS - exact) + 1e-9).astype(np.int64)
    bucket = np.where(n < exact, n, np.minimum(large, N_BUCKETS - 1))
    return (np.arange(N_BUCKETS)[:, None] == bucket[None, :]).astype(np.float32)


def hymba_layer(nc, x, w_in, lb_logits, hgrn_gnorm, rel_bias, w_o, norm_pre_mix, norm_post_mix,
                norm_pre_ffn, norm_post_ffn, w_gate, w_up, w_down, onehot, out):
    _, S, D = x.shape
    F = w_gate.shape[2]
    TB = S // P
    KT = D // P
    FT = F // P
    W = HEADS_A * DK
    TOP = min(TOPK_MAX, S // 4)
    assert (S, D, W, TB, KT, FT, TOP) == (512, 1024, 512, 4, 8, 22, 128)
    CH = KT * 256

    x_d, out_d = x[0], out[0]
    wi, wo, wg, wu, wd = w_in[0], w_o[0], w_gate[0], w_up[0], w_down[0]
    gscr = nc.dram_tensor("bias_by_distance", [HEADS_B, P, S + P], F32, kind="Internal").ap()

    SEG = {"f": W, "q": 0, "i": 2 * W, "g": 3 * W, "aq": 4 * W, "ak": 5 * W, "av": 6 * W, "iq": 7 * W}
    chunks = [("iq", 0), ("iq", 1), ("ikw", 0)]
    chunks += [(s, c) for s in ("f", "q", "i", "av", "g", "aq", "ak") for c in range(2)]
    J_WO = len(chunks)
    chunks += [("wo", c) for c in range(KT // 2)]
    J_FF = len(chunks)
    for c in range(FT // 2):
        chunks += [("gate", c), ("up", c)]
    J_DN = len(chunks)
    chunks += [("down", c) for c in range(FT // 2)]
    NCH = len(chunks)
    IKW = DH + HEADS_B

    groups = []
    for j in range(J_WO):
        for m in range(1 if chunks[j][0] == "ikw" else 2):
            groups.append((j, chunks[j][0], chunks[j][1], m))
    first_group = {}
    for g, (j, kind, c, m) in enumerate(groups):
        first_group.setdefault(kind, g)

    LEVELS = [64, 32, 16, 8, 4, 2, 1]
    G_L0 = first_group["i"] + 1
    LEVEL_AT = {G_L0 + l: l for l in range(len(LEVELS))}
    G_DIAG = G_L0 + len(LEVELS)
    G_ENDS, G_OFF, G_REC, G_YNORM, G_YTURN, G_YGATE = (G_DIAG + n for n in (1, 2, 3, 5, 9, 10))
    PAIRS = [(c, s) for c in range(TB) for s in range(c)]
    G_TOPK = first_group["f"] + 2
    UNITS = TB * HEADS_B
    DOTS = (TB - 1) * HEADS_B
    TURN_LAG, PV_LAG = 3, 5
    TURN_BANK = (4, 6, 2, 4)

    with ExitStack() as ctx:
        def sb(name, shape, dt=F32):
            return ctx.enter_context(nc.sbuf_tensor(name, shape, dt))

        def sem(name):
            return ctx.enter_context(nc.semaphore(name))

        PS = ctx.enter_context(nc.psum_tensor("PS", [P, 8, 512], F32))

        hT_hi = sb("hT_hi", [P, KT, S], F32R)
        hT_lo = sb("hT_lo", [P, KT, S], F32R)
        raw = sb("raw", [P, 2, CH])
        w_hi = sb("w_hi", [P, 2, CH], F32R)
        w_lo = sb("w_lo", [P, 2, CH], F32R)
        ident = sb("ident", [P, P])
        lmask = sb("lmask", [P, len(LEVELS), 64])
        M0 = sb("M0", [P, P])
        iw = sb("iw", [P, TB, HEADS_B])
        ss = sb("ss", [P, 40])
        ms = sb("ms", [P, 40])
        rstd = sb("rstd", [P, 40])
        mhalf = sb("mhalf", [P, 16])
        lbt = sb("lbt", [P, 2, HEADS_A])
        lbw = sb("lbw", [P, 6, HEADS_A])
        gn = sb("gn", [P, 1])
        eB = sb("eB", [P, HEADS_A, TB])
        top8 = sb("top8", [P, 8])
        mx = sb("mx", [P, UNITS])
        nm = sb("nm", [P, UNITS])
        sm = sb("sm", [P, UNITS])
        rs = sb("rs", [P, UNITS])

        N1, N2 = FT * 2 * S, 7936
        low = ExitStack()
        A1 = low.enter_context(nc.sbuf_tensor("A1", [P, N1], F32))
        low.close()
        with ExitStack() as low:
            low.enter_context(nc.sbuf_tensor("A1_front", [P, 6144], F32))
            QK = low.enter_context(nc.sbuf_tensor("QK", [P, 3, HEADS_B, S], F32R))
        ff = sb("ff", [P, FT, 2, S], F32R)
        A2 = sb("A2", [P, N2])

        def a1(o, n):
            return A1[:, o:o + n]

        QS, QX, KS = QK[:, 0], QK[:, 1], QK[:, 2]
        gT, ya, av = a1(0, 2048), a1(2048, 2048), a1(4096, 2048)
        gain_in, iwT = a1(4096, 1024), a1(5120, 512)
        V = a1(6144, 2048)
        Z = [a1(8192, 2048), a1(10240, 2048)]
        Sd = a1(12288, 2048).rearrange("p (c n) -> p c n", c=TB)
        So = a1(14336, 3072).rearrange("p (i n) -> p i n", i=len(PAIRS))
        UX, LX = a1(17408, 512), a1(17920, 512)
        xin = a1(18432, 4096).rearrange("p (t d) -> p t d", t=TB)
        rl = [a1(18432, 512), a1(18944, 512)]
        BM = [a1(18432 + 512 * i, 512) for i in range(2)]
        Pb = [a1(19456 + 512 * i, 512) for i in range(4)]
        PT = [a1(21504 + 512 * i, 512) for i in range(2)]
        yb = [a1(2048, 512), a1(2560, 512)]
        scr = [a1(6144, 1024), a1(7168, 1024)]
        qT, kT = A2[:, 0:2048], A2[:, 2048:4096]
        x2 = A2[:, 0:4096].rearrange("p (t d) -> p t d", t=TB)
        bT = A2[:, 4096:6144]
        oh_sb, tab, g_sb = A2[0:N_BUCKETS, 4096:4736], A2[0:N_BUCKETS, 4736:4744], A2[0:HEADS_B, 4768:5408]
        gain_mid = A2[:, 4096:6144].rearrange("p (a d) -> p a d", a=2)
        sig = [A2[:, 4096:4608], A2[:, 4608:5120]]
        fraw = [A2[:, 5120:5632], A2[:, 5632:6144]]
        SC = {1: A2[:, 6144:6400], 2: A2[:, 6400:6784], 3: A2[:, 6784:7296]}
        gain_out = A2[:, 6144:7168]
        Bh = A2[:, 0:4096].rearrange("p (h c) -> p h c", h=HEADS_B)
        junk = a1(18432, 1024)

        s_x = [sem(f"x_landed{t}") for t in range(TB)]
        s_gin = sem("gain_in_landed")
        s_small = sem("small_landed")
        s_raw = [sem(f"raw_landed{i}") for i in range(2)]
        s_hi = sem("w_hi_ready")
        s_lo = sem("w_lo_ready")
        STACKED = [g for g in range(len(groups)) if groups[g][1] in ("iq", "ikw", "aq", "ak")]
        s_rows = sem("row_chunk_used")
        s_ss = sem("sumsq_ready")
        s_rs = sem("rstd_ready")
        s_pool = sem("pool_chain")
        s_dve = sem("dve_chain")
        s_const = sem("const_ready")
        s_hx = sem("h_ready")
        s_hps = sem("hT_psum")
        s_hhi = sem("hT_hi_ready")
        s_hlo = sem("hT_lo_ready")
        s_proj = sem("proj_done")
        s_ev = [sem(f"proj_evacuated{b}") for b in range(4)]
        s_sig = sem("silu_sigmoid_ready")
        s_lbm = sem("lb_max_sub")
        s_lbe = sem("lb_exp")
        s_gps = sem("bias_row_psum")
        s_gsb = sem("bias_row_sbuf")
        s_gst = sem("bias_row_stored")
        s_bh = sem("bias_tile_landed")
        s_sth = sem("stack_hi_ready")
        s_iwp = sem("w_idx_psum")
        s_iws = sem("w_idx_ready")
        s_dot = sem("idx_dots")
        s_rl = sem("idx_relu")
        s_sc = sem("idx_score")
        s_fut = sem("score_causal")
        s_mask = sem("mask_ready")
        s_f = sem("forget_ready")
        s_ln = sem("log_f_ready")
        s_b = sem("cumsum_ready")
        s_rst = sem("scan_reset_ready")
        s_D = sem("level_exponent")
        s_E = sem("level_exp")
        s_Z = sem("level_operands")
        s_lvl = sem("level_scores_psum")
        s_ma = sem("level_merged")
        s_eb = sem("chunk_decay")
        s_off = sem("offdiag_psum")
        s_ofs = sem("offdiag_sbuf")
        s_o = sem("hgrn_o_psum")
        s_half = sem("half_of_squares")
        s_ya = sem("hgrn_o_sbuf")
        s_yn = sem("hgrn_y_normed")
        s_yt = sem("hgrn_yT_psum")
        s_yg = sem("hgrn_yT_gated")
        s_bm = sem("bias_mask")
        s_qk = sem("logits_psum")
        s_nm = sem("neg_max")
        s_ex = sem("exp_done")
        s_ptp = sem("probsT_psum")
        s_pts = [sem("probsT_sbuf_even"), sem("probsT_sbuf_odd")]
        s_pv = sem("pv_done")
        s_yb = sem("attention_y_normed")
        s_ybt = sem("attention_yT_psum")
        s_yhi = sem("yT_hi_ready")
        s_ylo = sem("yT_lo_ready")
        s_mid = sem("x_and_gains_landed")
        s_wo = sem("mix_out_psum")
        s_x2 = sem("x2_ready")
        s_gu = sem("gate_up_psum")
        s_fs = sem("gate_sigmoid")
        s_fr = sem("ff_raw_ready")
        s_fhi = sem("ff_hi_ready")
        s_flo = sem("ff_lo_ready")
        s_go = sem("gain_out_landed")
        s_dn = sem("down_psum")
        s_fin = sem("final_ready")
        s_out = sem("out_stored")

        def hb(t, h):
            return t[:, h * S:(h + 1) * S]

        def block_done(i):
            b, h = divmod(i - PV_LAG, HEADS_B)
            return b if h == HEADS_B - 1 and 0 <= b < TB - 1 else None

        def indexer_beside(g):
            n = (g - first_group["f"]) * KT - 6
            return range(min(max(n, 0), DOTS), min(max(n + KT, 0), DOTS))

        def last_of_chunk(g):
            return g + 1 == len(groups) or groups[g + 1][0] != groups[g][0]

        def evacuated(eng, g):
            eng.wait_ge(s_ev[g % 4], g // 4 + 1)

        NORMS = [("in", t) for t in range(TB)] + [("hgrn", 0), ("mix", 0), ("mix", 1), ("ffn", 0)]
        for t in range(2, TB):
            NORMS += [("mix", t), ("ffn", t - 1)]
        NORMS += [("ffn", TB - 1)] + [("out", t) for t in range(TB)]

        def norm(kind, t):
            return NORMS.index((kind, t)) + 1

        def turned_to_sbuf(eng, u, copy):
            n = (u // 8 + 1) * P
            eng.wait_ge(s_ptp, u + 1)
            if u >= 2:
                eng.wait_ge(s_pv, u - 1)
            copy(PT[u % 2][:, 0:n], PS[:, 2 + u % 2, 0:n]).then_inc(s_pts[u % 2], 1)

        def used(eng, j):
            if j < J_WO:
                eng.wait_ge(s_proj, sum(g[0] <= j for g in groups))
            elif j < J_FF:
                eng.wait_ge(*((s_wo, TB) if j == J_FF - 1 else (s_rows, j - J_WO + 1)))
            elif j < J_DN:
                eng.wait_ge(s_gu, 2 * (j - J_FF + 1))
            else:
                eng.wait_ge(s_rows, KT // 2 - 1 + j - J_DN + 1)

        def raw_src(j):
            kind, c = chunks[j]
            if kind == "ikw":
                return wi[:, 8 * W:8 * W + IKW].rearrange("(k p) n -> p k n", p=P)
            if kind in ("wo", "down"):
                src = wo if kind == "wo" else wd
                return src[c * 2 * P:(c + 1) * 2 * P, :].rearrange("(k p) n -> p k n", p=P)
            src = {"gate": wg, "up": wu}.get(kind, wi)
            lo = c * 256 + SEG.get(kind, 0)
            return src[:, lo:lo + 256].rearrange("(k p) n -> p k n", p=P)

        def slot(t, j):
            kind = chunks[j][0]
            if kind == "ikw":
                return t[:, j % 2, 0:KT * IKW].rearrange("p (k n) -> p k n", k=KT)
            return t[:, j % 2, :].rearrange("p (k n) -> p k n", k=2 if kind in ("wo", "down") else KT)

        def upper(t, z, c=None):
            return t.rearrange("p (n u z) -> p n u z", u=2, z=z)

        ctx.enter_context(nc.allow_non_contiguous_dma(reason="lower bounds and group gains go one per partition"))
        block = ctx.enter_context(nc.Block())

        @block.sync
        def _(sp):
            for t in range(TB):
                sp.dma_start(xin[:, t, :], x_d[t * P:(t + 1) * P, :]).then_inc(s_x[t], 16)
                if t == 0:
                    sp.dma_start(gain_in, norm_pre_mix[0, :].partition_broadcast(P)).then_inc(s_gin, 16)
            for j in range(NCH):
                if j >= 2:
                    sp.wait_ge(s_lo, j - 1)
                sp.dma_start(slot(raw, j), raw_src(j)).then_inc(s_raw[j % 2], 16)
            for t in range(TB):
                for half in range(2):
                    c = slice(half * 512, (half + 1) * 512)
                    sp.wait_ge(s_fin, 2 * t + half + 1)
                    sp.dma_start(out_d[t * P:(t + 1) * P, c], x2[:, t, c]).then_inc(s_out, 16)
            sp.wait_ge(s_out, 16 * 2 * TB)

        @block.gpsimd
        def _(pool):
            n_chain = [0]

            def link(ins):
                n_chain[0] += 1
                ins.then_inc(s_pool, 1)
                pool.wait_ge(s_pool, n_chain[0])

            def inv_root(col, n, width):
                link(pool.tensor_scalar(ms[:, col:col + n], ss[:, col:col + n], 1.0 / width, EPS, ALU.mult, ALU.add))
                pool.tensor_tensor(rstd[:, col:col + n], ms[:, col:col + n], mhalf[:, 0:n], ALU.pow).then_inc(s_rs, 1)

            link(pool.memset(ident[:, :], 0.0))
            pool.affine_select(out=ident[:, :], in_=ident[:, :], compare_op=ALU.not_equal, fill=1.0, base=0,
                               pattern=[[-1, P]], channel_multiplier=1).then_inc(s_const, 1)
            link(pool.memset(mhalf[:, :], -0.5))
            for t in range(TB):
                pool.wait_ge(s_ss, norm("in", t))
                inv_root(t, 1, D)
            link(pool.memset(lmask[:, :, :], 1.0))
            for l, z in enumerate(LEVELS):
                v = lmask[:, l, :].rearrange("p (n z) -> p n z", z=z)
                link(pool.affine_select(out=v, in_=v, compare_op=ALU.is_ge, fill=0.0, base=0,
                                        pattern=[[-2 * z, 64 // z], [0, z]], channel_multiplier=1))
                link(pool.affine_select(out=v, in_=v, compare_op=ALU.is_ge, fill=0.0, base=z - 1,
                                        pattern=[[2 * z, 64 // z], [0, z]], channel_multiplier=-1))
            link(pool.memset(M0[:, :], 0.0))
            pool.affine_select(out=M0[:, :], in_=M0[:, :], compare_op=ALU.is_ge, fill=CLOSED, base=0,
                               pattern=[[-1, P]], channel_multiplier=1).then_inc(s_const, 1)
            for b in (1, 2, 3):
                pool.wait_ge(s_sc, 8 * b)
                v = SC[b][:, b * P:(b + 1) * P]
                pool.affine_select(out=v, in_=v, compare_op=ALU.is_ge, fill=FUTURE, base=0,
                                   pattern=[[-1, P]], channel_multiplier=1).then_inc(s_fut, 1)
            pool.wait_ge(s_dot, DOTS)
            pool.memset(Sd[:, :, :], 0.0).then_inc(s_const, 1)
            link(pool.memset(Z[1], 1.0))
            pool.memset(Z[1].rearrange("p (n t) -> p n t", t=P)[:, :, 0:1], 0.0).then_inc(s_rst, 1)
            pool.wait_ge(s_b, 1)
            for l, z in enumerate(LEVELS):
                if l >= 2:
                    pool.wait_ge(s_lvl, 4 * (l - 1))
                b4 = upper(bT, z)
                d4 = upper(Z[l % 2], z)
                edge = b4[:, :, 0, z - 1:z].to_broadcast([P, S * HEADS_A // (2 * z), z])
                pool.tensor_tensor(d4[:, :, 1, :], b4[:, :, 1, :], edge, ALU.subtract)
                pool.tensor_tensor(d4[:, :, 0, :], edge, b4[:, :, 0, :], ALU.subtract).then_inc(s_D, 1)
            pool.wait_ge(s_lvl, 4 * len(LEVELS))
            b3 = bT.rearrange("p (n t) -> p n t", t=P)
            end = b3[:, :, P - 1:P].to_broadcast([P, HEADS_A * TB, P])
            pool.tensor_tensor(Z[0].rearrange("p (n t) -> p n t", t=P), end, b3, ALU.subtract).then_inc(s_D, 1)
            pool.wait_ge(s_gst, 16)
            pool.wait_ge(s_lvl, 4 * (len(LEVELS) + 1))
            pool.wait_ge(s_Z, len(LEVELS) + 2)
            for h in range(HEADS_B):
                pool.dma_start(Bh[:, h, :], bass.AP(tensor=gscr.tensor, offset=h * P * (S + P) + P - 1,
                                                    ap=[[S + P - 1, P], [1, S]])).then_inc(s_bh, 16)
            pool.wait_ge(s_E, len(LEVELS) + 2)
            pool.wait_ge(s_eb, 1)
            for a, gain in enumerate((norm_post_mix, norm_pre_ffn)):
                pool.dma_start(gain_mid[:, a, :], gain[0, :].partition_broadcast(P)).then_inc(s_mid, 16)
            pool.wait_ge(s_ss, norm("hgrn", 0))
            inv_root(16, 16, DK)
            pool.wait_ge(s_bh, 16 * HEADS_B)
            for u in range(UNITS):
                b, h = divmod(u, HEADS_B)
                n = (b + 1) * P
                if h == 0 and b:
                    pool.wait_ge(s_mask, b)
                if u >= 2:
                    pool.wait_ge(s_nm, u - 1)
                M = M0[:, :] if b == 0 else SC[b]
                pool.tensor_tensor(BM[u % 2][:, 0:n], Bh[:, h, (TB - 1 - b) * P:S], M, ALU.add).then_inc(s_bm, 1)
            pool.wait_ge(s_bm, UNITS)
            for t in range(TB):
                pool.dma_start(x2[:, t, :], x_d[t * P:(t + 1) * P, :]).then_inc(s_mid, 16)
            for k in range(TB + 1):
                if k < TB:
                    pool.wait_ge(s_ss, norm("mix", k))
                    inv_root(4 + k, 1, D)
                if k >= 1:
                    pool.wait_ge(s_ss, norm("ffn", k - 1))
                    inv_root(8 + k - 1, 1, D)
            pool.dma_start(gain_out, norm_post_ffn[0, :].partition_broadcast(P)).then_inc(s_go, 16)
            for t in range(TB):
                pool.wait_ge(s_ss, norm("out", t))
                inv_root(12 + t, 1, D)

        @block.scalar
        def _(act):
            def split(j):
                act.wait_ge(s_raw[j % 2], 16 * (j // 2 + 1))
                if j >= 2:
                    used(act, j - 2)
                act.activation(slot(w_hi, j), slot(raw, j), ACT.Copy).then_inc(s_hi, 1)

            def turn_hi(n, banks, t):
                act.wait_ge(s_hps, n + 1)
                act.activation(hT_hi[:, :, t * P:(t + 1) * P],
                               PS[:, banks:banks + 2, :].rearrange("p a (k t) -> p (a k) t", t=P),
                               ACT.Copy).then_inc(s_hhi, 1)

            act.dma_start(lbt[:, :, :], lb_logits.rearrange("r (h p) -> p r h", p=P)).then_inc(s_small, 16)
            act.dma_start(gn[:, :], hgrn_gnorm.rearrange("a p -> p a")).then_inc(s_small, 16)
            act.dma_start(tab, rel_bias).then_inc(s_small, 16)
            act.dma_start(oh_sb, onehot).then_inc(s_small, 16)
            for t in range(TB):
                act.wait_ge(s_x[t], 16)
                if t:
                    act.wait_ge(s_ss, t)
                act.activation(ya[:, 0:D], xin[:, t, :], ACT.Square, accum_out=ss[:, t:t + 1]).then_inc(s_ss, 1)
            act.wait_ge(s_gps, 1)
            act.activation(g_sb[:, 0:S], PS[0:HEADS_B, 0, :], ACT.Copy)
            act.activation(g_sb[:, S:S + P], PS[0:HEADS_B, 1, 0:P], ACT.Copy).then_inc(s_gsb, 1)
            act.wait_ge(s_lbm, 1)
            act.activation(lbw[:, 1:3, :], lbt[:, :, :], ACT.Exp).then_inc(s_lbe, 1)
            for t in range(TB):
                turn_hi(t, TURN_BANK[t], t)
                if t == 1:
                    split(0)
            split(1)
            act.wait_ge(s_gsb, 1)
            act.dma_start(gscr, g_sb.unsqueeze(1).to_broadcast([HEADS_B, P, S + P])).then_inc(s_gst, 16)

            def evac(g):
                j, kind, c, m = groups[g]
                act.wait_ge(s_proj, g + 1)
                ps = PS[:, g % 4, :]
                done = s_ev[g % 4]
                h = 2 * c + m
                if kind in ("iq", "aq"):
                    if kind == "aq":
                        act.wait_ge(s_o, TB)
                    for e in range(2):
                        scale = DH ** -0.5 if kind == "aq" else 1.0
                        act.activation(QS[0:DH, 2 * h + e, :], ps[e * DH:(e + 1) * DH, :], ACT.Copy, scale=scale)
                        o = act.activation(QX[DH:P, 2 * h + e, :], ps[e * DH:(e + 1) * DH, :], ACT.Copy, scale=scale)
                    o.then_inc(s_sth, 1)
                elif kind == "ak":
                    for e in range(2):
                        o = act.activation(KS[0:DH, 2 * h + e, :], ps[e * DH:(e + 1) * DH, :], ACT.Copy)
                    o.then_inc(s_sth, 1)
                elif kind == "ikw":
                    act.wait_ge(s_hx, TB)
                    act.activation(KS[0:DH, 0, :], ps[0:DH, :], ACT.Copy)
                    act.activation(iwT[DH:IKW, :], ps[DH:IKW, :], ACT.Copy).then_inc(s_sth, 1)
                elif kind == "f":
                    if g == first_group["f"]:
                        act.wait_ge(s_gst, 16)
                    act.activation(hb(kT, h), ps, ACT.Sigmoid).then_inc(done, 1)
                elif kind in ("q", "g"):
                    act.activation(hb(qT if kind == "q" else gT, h), ps, ACT.Sigmoid).then_inc(s_sig, 1)
                else:
                    dst = (V if kind == "i" else av).rearrange("p (t n) -> p t n", t=TB)
                    act.activation(dst[:, 2 * m:2 * m + 2, c * 256:(c + 1) * 256],
                                   ps.rearrange("p (t n) -> p t n", t=2), ACT.Copy).then_inc(done, 1)

            def level_exp(l):
                act.wait_ge(s_D, l + 1)
                act.activation(Z[l % 2], Z[l % 2], ACT.Exp).then_inc(s_E, 1)

            for g, (j, kind, c, m) in enumerate(groups):
                if g in LEVEL_AT:
                    level_exp(LEVEL_AT[g])
                for u in indexer_beside(g):
                    n = (u // 8 + 2) * P
                    act.wait_ge(s_dot, u + 1)
                    if u >= 2:
                        act.wait_ge(s_sc, u - 1)
                    act.activation(rl[u % 2][:, 0:n], PS[:, 4 + u % 2, 0:n], ACT.Relu).then_inc(s_rl, 1)
                evac(g)
                if last_of_chunk(g) and j + 2 <= J_WO:
                    split(j + 2)
                if g == first_group["q"] - 1:
                    act.wait_ge(s_f, 1)
                    act.activation(Z[0], bT, ACT.Ln).then_inc(s_ln, 1)
                if g == G_DIAG:
                    b4 = bT.rearrange("p (h c t) -> p h c t", h=HEADS_A, c=TB)
                    act.activation(eB[:, :, :], b4[:, :, :, P - 1], ACT.Exp).then_inc(s_eb, 1)
                    act.wait_ge(s_lvl, 4 * (len(LEVELS) - 1))
                    act.activation(Z[1], bT, ACT.Exp).then_inc(s_E, 1)
                    act.wait_ge(s_D, len(LEVELS) + 1)
                    act.activation(Z[0], Z[0], ACT.Exp).then_inc(s_E, 1)
                if g == G_OFF:
                    for i in range(len(PAIRS)):
                        act.wait_ge(s_off, i + 1)
                        act.activation(So[:, i, :], PS[:, 4 + i % 4, :], ACT.Copy).then_inc(s_ofs, 1)
                if g == G_YNORM:
                    act.wait_ge(s_ya, TB)
                    for i in range(16):
                        if i == 8:
                            o.then_inc(s_half, 1)
                            act.wait_ge(s_half, 1)
                        o = act.activation(junk[:, i % 8 * DK:(i % 8 + 1) * DK], ya[:, i * DK:(i + 1) * DK],
                                           ACT.Square, accum_out=ss[:, 16 + i:17 + i])
                    o.then_inc(s_ss, 1)

            def y_hi_a():
                act.wait_ge(s_yg, TB)
                used(act, J_WO - 1)
                act.activation(hT_hi[:, 0:4, :], gT.rearrange("p (h t) -> p h t", t=S), ACT.Copy).then_inc(s_yhi, 1)

            def y_hi_b(b):
                act.wait_ge(s_ybt, b + 1)
                act.activation(hT_hi[:, 4:8, b * P:(b + 1) * P],
                               PS[:, 6 + b % 2, :].rearrange("p (k t) -> p k t", t=P), ACT.Copy).then_inc(s_yhi, 1)

            for i in range(UNITS + PV_LAG):
                if i < UNITS:
                    n = (i // 8 + 1) * P
                    act.wait_ge(s_nm, i + 1)
                    act.activation(Pb[i % 4][:, 0:n], Pb[i % 4][:, 0:n], ACT.Exp, bias=nm[:, i:i + 1],
                                   accum_out=sm[:, i:i + 1]).then_inc(s_ex, 1)
                if (i - TURN_LAG) % 2 == 0 and TURN_LAG <= i < UNITS + TURN_LAG:
                    turned_to_sbuf(act, i - TURN_LAG, lambda o, p: act.activation(o, p, ACT.Copy))
                if i == 2:
                    y_hi_a()
                if i == 7:
                    split(J_WO + 1)
                b = block_done(i - 3)
                if b is not None:
                    y_hi_b(b)
            y_hi_b(TB - 1)
            split(J_WO + 2)
            split(J_WO + 3)
            split(J_WO + 4)
            for k in range(TB + 2):
                if k < TB:
                    act.wait_ge(s_wo, k + 1)
                    act.wait_ge(s_ss, norm("mix", k) - 1)
                    act.activation(junk, PS[:, 2 * k:2 * k + 2, :].rearrange("p a n -> p (a n)"),
                                   ACT.Square, accum_out=ss[:, 4 + k:5 + k]).then_inc(s_ss, 1)
                if 1 <= k <= TB:
                    act.wait_ge(s_x2, k)
                    act.wait_ge(s_ss, norm("ffn", k - 1) - 1)
                    act.activation(junk, x2[:, k - 1, :], ACT.Square, accum_out=ss[:, 7 + k:8 + k]).then_inc(s_ss, 1)
                if k >= 2:
                    turn_hi(TB + k - 2, 2 * (k - 2), k - 2)
            split(J_FF + 1)
            for i in range(FT // 2):
                split(J_FF + 2 * i + 2)
                for f in (2 * i, 2 * i + 1):
                    act.wait_ge(s_gu, 2 * (f // 2) * 2 + (f % 2) + 1)
                    if f >= 2:
                        act.wait_ge(s_fr, f - 1)
                    act.activation(sig[f % 2], PS[:, f % 2, :], ACT.Sigmoid).then_inc(s_fs, 1)
                act.wait_ge(s_fr, 2 * i + 1)
                act.activation(ff[:, 2 * i, 0, :], fraw[0], ACT.Copy).then_inc(s_fhi, 1)
                split(J_FF + 2 * i + 3)
                act.wait_ge(s_fr, 2 * i + 2)
                act.activation(ff[:, 2 * i + 1, 0, :], fraw[1], ACT.Copy).then_inc(s_fhi, 1)
            for j in range(J_DN + 2, NCH):
                split(j)
            for t in range(TB):
                act.wait_ge(s_dn, t + 1)
                act.wait_ge(s_ss, norm("out", t) - 1)
                act.activation(raw[:, t % 2, 0:D], PS[:, 2 * t:2 * t + 2, :].rearrange("p a n -> p (a n)"),
                               ACT.Square, accum_out=ss[:, 12 + t:13 + t]).then_inc(s_ss, 1)

        @block.vector
        def _(dve):
            n_chain = [0]

            def link(ins):
                n_chain[0] += 1
                ins.then_inc(s_dve, 1)
                dve.wait_ge(s_dve, n_chain[0])

            def split(j):
                dve.wait_ge(s_hi, j + 1)
                dve.tensor_tensor(slot(w_lo, j), slot(raw, j), slot(w_hi, j).bitcast(F32),
                                  ALU.subtract).then_inc(s_lo, 1)

            def turn_lo(n, banks, t):
                dve.wait_ge(s_hhi, n + 1)
                dve.tensor_tensor(hT_lo[:, :, t * P:(t + 1) * P],
                                  PS[:, banks:banks + 2, :].rearrange("p a (k t) -> p (a k) t", t=P),
                                  hT_hi[:, :, t * P:(t + 1) * P].bitcast(F32), ALU.subtract).then_inc(s_hlo, 1)

            dve.wait_ge(s_small, 64)
            link(dve.tensor_tensor(lbw[:, 0, :], lbt[:, 0, :], lbt[:, 1, :], ALU.max))
            for r in range(2):
                o = dve.tensor_tensor(lbt[:, r, :], lbt[:, r, :], lbw[:, 0, :], ALU.subtract)
            o.then_inc(s_lbm, 1)
            dve.wait_ge(s_gin, 16)
            for t in range(TB):
                dve.wait_ge(s_rs, norm("in", t))
                dve.scalar_tensor_tensor(out=xin[:, t, :], in0=xin[:, t, :], scalar=rstd[:, t:t + 1], in1=gain_in,
                                         op0=ALU.mult, op1=ALU.mult).then_inc(s_hx, 1)
            for t in range(TB):
                turn_lo(t, TURN_BANK[t], t)
                if t == 1:
                    split(0)
            split(1)
            dve.wait_ge(s_lbe, 1)
            link(dve.tensor_tensor(lbw[:, 3, :], lbw[:, 1, :], lbw[:, 2, :], ALU.add))
            link(dve.reciprocal(lbw[:, 3, :], lbw[:, 3, :]))
            link(dve.tensor_tensor(lbw[:, 4, :], lbw[:, 1, :], lbw[:, 3, :], ALU.mult))
            link(dve.tensor_scalar(lbw[:, 5, :], lbw[:, 4, :], -1.0, 1.0, ALU.mult, ALU.add))

            def silu_mul(g):
                j, kind, c, m = groups[g]
                n_sig = g - first_group["q"] if kind == "q" else g - first_group["g"] + 4
                dve.wait_ge(s_sig, n_sig + 1)
                dst = hb(qT if kind == "q" else gT, 2 * c + m)
                dve.tensor_tensor(dst, PS[:, g % 4, :], dst, ALU.mult).then_inc(s_ev[g % 4], 1)

            def topk_round(r):
                b, k = r // 16 + 1, r % 16
                if k == 0:
                    dve.wait_ge(s_fut, b)
                link(dve.max(top8[:, :], SC[b]))
                link(dve.match_replace(SC[b], top8[:, :], SC[b], TAKEN))
                if k == 15:
                    dve.tensor_scalar(SC[b], SC[b], 0.5 * (FUTURE + TAKEN), CLOSED, ALU.is_gt,
                                      ALU.mult).then_inc(s_mask, 1)

            rounds = iter(range(48))

            def topk_rounds(n):
                for _, r in zip(range(n), rounds):
                    topk_round(r)

            def merge(l):
                z = LEVELS[l]
                if l:
                    dve.wait_ge(s_ma, 4 * l)
                for c in range(TB):
                    dve.wait_ge(s_lvl, 4 * l + c + 1)
                    v = Sd[:, c, :].rearrange("p (h n u z) -> p h n u z", h=HEADS_A, u=2, z=z)[:, :, :, 1, :]
                    s = PS[:, 4 + c, :].rearrange("p (h n u z) -> p h n u z", h=HEADS_A, u=2, z=z)[:, :, :, 1, :]
                    m = lmask[:, l, :].rearrange("p (n z) -> p n z", z=z).bitcast(U32)
                    m = m.unsqueeze(1).to_broadcast([P, HEADS_A, 64 // z, z])
                    dve.copy_predicated(v, m, s).then_inc(s_ma, 1)

            def chunk_ends():
                dve.wait_ge(s_E, len(LEVELS) + 1)
                link(dve.tensor_tensor(Z[1], Z[1], qT, ALU.mult))
                dve.wait_ge(s_E, len(LEVELS) + 2)
                link(dve.tensor_tensor(Z[0], Z[0], kT, ALU.mult))
                dve.wait_ge(s_eb, 1)
                for h in range(HEADS_A):
                    dve.tensor_scalar(UX[:, h * P:(h + 1) * P], hb(Z[1], h)[:, 3 * P:4 * P], eB[:, h, 2:3], None,
                                      ALU.mult)
                    o = dve.tensor_scalar(LX[:, h * P:(h + 1) * P], hb(Z[0], h)[:, 0:P], eB[:, h, 1:2], None,
                                          ALU.mult)
                o.then_inc(s_Z, 2)

            def diagonal():
                dve.wait_ge(s_ma, 4 * len(LEVELS))
                for c in range(TB):
                    dve.wait_ge(s_lvl, 4 * len(LEVELS) + c + 1)
                    dve.copy_predicated(Sd[:, c, :].rearrange("p (h t) -> p h t", t=P),
                                        ident[:, :].bitcast(U32).unsqueeze(1).to_broadcast([P, HEADS_A, P]),
                                        PS[:, 4 + c, :].rearrange("p (h t) -> p h t", t=P)).then_inc(s_ma, 1)

            def y_norm():
                dve.wait_ge(s_rs, norm("hgrn", 0))
                v = ya.rearrange("p (n d) -> p n d", d=DK)
                dve.tensor_tensor(v, v, rstd[:, 16:32].unsqueeze(2).to_broadcast([P, 16, DK]),
                                  ALU.mult).then_inc(s_yn, 1)

            def y_gate():
                for h in range(HEADS_A):
                    evacuated(dve, first_group["g"] + h)
                for t in range(TB):
                    dve.wait_ge(s_yt, t + 1)
                    v = gT.rearrange("p (h t) -> p h t", t=S)[:, :, t * P:(t + 1) * P]
                    dve.scalar_tensor_tensor(out=v, in0=PS[:, 4 + t, :].rearrange("p (h t) -> p h t", t=P),
                                             scalar=gn[:, 0:1], in1=v, op0=ALU.mult, op1=ALU.mult).then_inc(s_yg, 1)

            def stack_lo(g):
                j, kind, c, m = groups[g]
                dve.wait_ge(s_sth, STACKED.index(g) + 1)
                ps = PS[:, g % 4, :]
                h = 2 * c + m
                scale = DH ** -0.5 if kind == "aq" else 1.0
                for e in range(1 if kind == "ikw" else 2):
                    p, i = ps[e * DH:(e + 1) * DH, :], 0 if kind == "ikw" else 2 * h + e
                    if kind in ("iq", "aq"):
                        hi = (QX[DH:P, i, :] if e else QS[0:DH, i, :]).bitcast(F32)
                        outs = (QS[DH:P, i, :], QX[0:DH, i, :])
                    else:
                        hi, outs = KS[0:DH, i, :].bitcast(F32), (KS[DH:P, i, :],)
                    for t in outs:
                        o = dve.scalar_tensor_tensor(out=t, in0=p, scalar=scale, in1=hi, op0=ALU.mult,
                                                     op1=ALU.subtract)
                o.then_inc(s_ev[g % 4], 1)

            def evac(g):
                if g in STACKED:
                    stack_lo(g)
                elif groups[g][1] in ("q", "g"):
                    silu_mul(g)

            def level_operands(l):
                z = LEVELS[l]
                dve.wait_ge(s_E, l + 1)
                if l == 0:
                    for h in range(HEADS_A):
                        evacuated(dve, first_group["q"] + h)
                z4 = upper(Z[l % 2], z)
                dve.tensor_tensor(z4[:, :, 1, :], z4[:, :, 1, :], upper(qT, z)[:, :, 1, :], ALU.mult)
                dve.tensor_tensor(z4[:, :, 0, :], z4[:, :, 0, :], upper(kT, z)[:, :, 0, :],
                                  ALU.mult).then_inc(s_Z, 1)

            for g, (j, kind, _, m) in enumerate(groups):
                if g in LEVEL_AT:
                    level_operands(LEVEL_AT[g])
                if g == G_ENDS:
                    chunk_ends()
                for u in indexer_beside(g):
                    b, h = u // 8 + 1, u % 8
                    n = (b + 1) * P
                    if u == 0:
                        dve.wait_ge(s_iwp, 1)
                        dve.tensor_scalar(iw[:, :, :], PS[:, 6, 0:TB * HEADS_B].rearrange("p (t h) -> p t h", t=TB),
                                          HEADS_B ** -0.5 * DH ** -0.5, None, ALU.mult).then_inc(s_iws, 1)
                        dve.wait_ge(s_iws, 1)
                    dve.wait_ge(s_rl, u + 1)
                    if h == 0:
                        o = dve.tensor_scalar(SC[b], rl[u % 2][:, 0:n], iw[:, b, h:h + 1], None, ALU.mult)
                    else:
                        dve.wait_ge(s_sc, u)
                        o = dve.scalar_tensor_tensor(out=SC[b], in0=rl[u % 2][:, 0:n], scalar=iw[:, b, h:h + 1],
                                                     in1=SC[b], op0=ALU.mult, op1=ALU.add)
                    o.then_inc(s_sc, 1)
                evac(g)
                if g >= G_TOPK:
                    topk_rounds(2 if g < G_L0 - 4 or g > G_REC else 1)
                if g == first_group["q"] - 1:
                    for h in range(HEADS_A):
                        evacuated(dve, first_group["f"] + h)
                        o = dve.tensor_scalar(hb(bT, h), hb(kT, h), lbw[:, 5, h:h + 1], lbw[:, 4, h:h + 1],
                                              ALU.mult, ALU.add)
                    link(o)
                    dve.tensor_scalar(kT, bT, -1.0, 1.0, ALU.mult, ALU.add).then_inc(s_f, 1)
                elif g == first_group["q"] + 1:
                    dve.wait_ge(s_ln, 1)
                    dve.wait_ge(s_rst, 1)
                    dve.tensor_tensor_scan(bT, Z[1], Z[0], 0.0, ALU.mult, ALU.add).then_inc(s_b, 1)
                if g in LEVEL_AT:
                    if g == G_L0:
                        dve.wait_ge(s_const, 3)
                    merge(LEVEL_AT[g])
                elif g == G_DIAG:
                    diagonal()
                elif g == G_REC:
                    for c in range(TB):
                        dve.wait_ge(s_o, c + 1)
                        dve.tensor_copy(ya[:, c * W:(c + 1) * W], PS[:, 4 + c, :]).then_inc(s_ya, 1)
                elif g == G_YNORM + 1:
                    y_norm()
                elif g == G_YGATE:
                    y_gate()
                if last_of_chunk(g) and j + 2 <= J_WO:
                    split(j + 2)
                if g >= G_TOPK:
                    topk_rounds(1)
            topk_rounds(48)

            def y_lo_a():
                dve.wait_ge(s_yhi, 1)
                dve.tensor_tensor(hT_lo[:, 0:4, :], gT.rearrange("p (h t) -> p h t", t=S),
                                  hT_hi[:, 0:4, :].bitcast(F32), ALU.subtract).then_inc(s_ylo, 1)

            def y_lo_b(b):
                dve.wait_ge(s_yhi, b + 2)
                dve.tensor_tensor(hT_lo[:, 4:8, b * P:(b + 1) * P],
                                  PS[:, 6 + b % 2, :].rearrange("p (k t) -> p k t", t=P),
                                  hT_hi[:, 4:8, b * P:(b + 1) * P].bitcast(F32), ALU.subtract).then_inc(s_ylo, 1)

            def y_norm_b(b):
                u = slice(8 * b, 8 * b + 8)
                dve.wait_ge(s_ex, 8 * b + 8)
                link(dve.reciprocal(rs[:, u], sm[:, u]))
                dve.wait_ge(s_pv, 8 * b + 8)
                if b >= 2:
                    dve.wait_ge(s_ybt, b - 1)
                dve.tensor_tensor(yb[b % 2].rearrange("p (h d) -> p h d", d=DH),
                                  PS[:, 4 + b % 2, :].rearrange("p (h d) -> p h d", d=DH),
                                  rs[:, u].unsqueeze(2).to_broadcast([P, HEADS_B, DH]), ALU.mult).then_inc(s_yb, 1)

            for i in range(UNITS + PV_LAG):
                if i < UNITS:
                    n = (i // 8 + 1) * P
                    dve.wait_ge(s_qk, i + 1)
                    dve.wait_ge(s_bm, i + 1)
                    if i >= 4:
                        dve.wait_ge(s_ptp, i - 3)
                    link(dve.tensor_tensor_reduce(Pb[i % 4][:, 0:n], PS[:, i % 2, 0:n], BM[i % 2][:, 0:n], 1.0,
                                                  -3.4e38, ALU.add, ALU.max, mx[:, i:i + 1]))
                    dve.tensor_scalar(nm[:, i:i + 1], mx[:, i:i + 1], -1.0, None, ALU.mult).then_inc(s_nm, 1)
                if (i - TURN_LAG) % 2 == 1 and TURN_LAG <= i < UNITS + TURN_LAG:
                    turned_to_sbuf(dve, i - TURN_LAG, dve.tensor_copy)
                if i == 4:
                    y_lo_a()
                if i == 8:
                    split(J_WO + 1)
                b = block_done(i - 1)
                if b is not None:
                    y_norm_b(b)
                b = block_done(i - 3)
                if b is not None:
                    y_lo_b(b)
            y_norm_b(TB - 1)
            y_lo_b(TB - 1)
            split(J_WO + 2)
            split(J_WO + 3)
            split(J_WO + 4)
            dve.wait_ge(s_mid, 16 * 6)
            for k in range(TB + 2):
                if k < TB:
                    dve.wait_ge(s_ss, norm("mix", k))
                    if k >= 2:
                        dve.wait_ge(s_hps, TB + k - 1)
                    link(dve.tensor_tensor(scr[k % 2], PS[:, 2 * k:2 * k + 2, :].rearrange("p a n -> p (a n)"),
                                           gain_mid[:, 0, :], ALU.mult))
                    dve.wait_ge(s_rs, norm("mix", k))
                    dve.scalar_tensor_tensor(out=x2[:, k, :], in0=scr[k % 2], scalar=rstd[:, 4 + k:5 + k],
                                             in1=x2[:, k, :], op0=ALU.mult, op1=ALU.add).then_inc(s_x2, 1)
                if 1 <= k <= TB:
                    dve.wait_ge(s_rs, norm("ffn", k - 1))
                    dve.wait_ge(s_x2, k)
                    dve.scalar_tensor_tensor(out=scr[(k - 1) % 2], in0=x2[:, k - 1, :], scalar=rstd[:, 7 + k:8 + k],
                                             in1=gain_mid[:, 1, :], op0=ALU.mult, op1=ALU.mult).then_inc(s_hx, 1)
                if k >= 2:
                    turn_lo(TB + k - 2, 2 * (k - 2), k - 2)
            split(J_FF + 1)

            def ff_mul(f):
                dve.wait_ge(s_fs, f + 1)
                link(dve.tensor_tensor(sig[f % 2], PS[:, f % 2, :], sig[f % 2], ALU.mult))
                dve.wait_ge(s_gu, 4 * (f // 2) + 2 + f % 2 + 1)
                if f >= 2:
                    dve.wait_ge(s_fhi, f - 1)
                dve.tensor_tensor(fraw[f % 2], PS[:, 2 + f % 2, :], sig[f % 2], ALU.mult).then_inc(s_fr, 1)

            def ff_lo(f):
                dve.wait_ge(s_fhi, f + 1)
                dve.tensor_tensor(ff[:, f, 1, :], fraw[f % 2], ff[:, f, 0, :].bitcast(F32),
                                  ALU.subtract).then_inc(s_flo, 1)

            for i in range(FT // 2):
                split(J_FF + 2 * i + 2)
                ff_mul(2 * i)
                ff_lo(2 * i)
                ff_mul(2 * i + 1)
                split(J_FF + 2 * i + 3)
                ff_lo(2 * i + 1)
            for j in range(J_DN + 2, NCH):
                split(j)
            dve.wait_ge(s_go, 16)
            for t in range(TB):
                dve.wait_ge(s_ss, norm("out", t))
                o = raw[:, t % 2, D:2 * D]
                link(dve.tensor_tensor(o, PS[:, 2 * t:2 * t + 2, :].rearrange("p a n -> p (a n)"), gain_out, ALU.mult))
                dve.wait_ge(s_rs, norm("out", t))
                for half in range(2):
                    c = slice(half * 512, (half + 1) * 512)
                    dve.scalar_tensor_tensor(out=x2[:, t, c], in0=o[:, c], scalar=rstd[:, 12 + t:13 + t],
                                             in1=x2[:, t, c], op0=ALU.mult, op1=ALU.add).then_inc(s_fin, 1)

        @block.tensor
        def _(pe):
            def passes(k, lhs, rhs, out, first, last):
                for n, (a, b) in enumerate(((0, 1), (1, 0), (0, 0))):
                    o = pe.matmul(out, lhs[a], rhs[b], start=(first and n == 0), stop=(last and n == 2))
                return o

            def weights(j):
                return slot(w_hi, j), slot(w_lo, j)

            def feature_group(w, m, M, bank, lo, hi, done, beside=None):
                for k in range(KT):
                    o = passes(k, [x[:, k, m * M:(m + 1) * M] for x in w],
                               [hT[:, k, lo:hi] for hT in (hT_hi, hT_lo)], PS[0:M, bank, lo:hi],
                               k == 0, k == KT - 1)
                    if k == KT - 1 and done is not None:
                        o.then_inc(done, 1)
                    if beside:
                        beside(k)

            def project(g):
                j, kind, _, m = groups[g]
                pe.wait_ge(s_lo, j + 1)
                w = weights(j)
                if g >= 4:
                    evacuated(pe, g - 4)
                if kind in ("i", "av"):
                    for tt in range(2):
                        t = 2 * m + tt
                        for k in range(KT):
                            o = passes(k, [hT[:, k, t * P:(t + 1) * P] for hT in (hT_hi, hT_lo)],
                                       [x[:, k, :] for x in w], PS[:, g % 4, tt * 256:(tt + 1) * 256],
                                       k == 0, k == KT - 1)
                    o.then_inc(s_proj, 1)
                else:
                    feature_group(w, m, IKW if kind == "ikw" else P, g % 4, 0, S, s_proj,
                                  (lambda k: indexer_dot(g, k)) if len(indexer_beside(g)) else None)

            def turn(src, bank):
                for k in range(KT):
                    o = pe.transpose(PS[:, bank + k // 4, (k % 4) * P:(k % 4 + 1) * P],
                                     src[:, k * P:(k + 1) * P], ident[:, :])
                o.then_inc(s_hps, 1)

            def stacked_dots(out, b, h, kh):
                pe.matmul(out, QS[:, h, b * P:(b + 1) * P], KS[:, kh, 0:(b + 1) * P], start=True, stop=False)
                return pe.matmul(out, QX[:, h, b * P:(b + 1) * P], KS[:, kh, 0:(b + 1) * P], start=False, stop=True)

            def indexer_dot(g, k):
                u = (g - first_group["f"]) * KT + k - 6
                if u == 0:
                    evacuated(pe, first_group["ikw"])
                    for t in range(TB):
                        o = pe.transpose(PS[:, 6, t * HEADS_B:(t + 1) * HEADS_B], iwT[DH:IKW, t * P:(t + 1) * P],
                                         ident[DH:IKW, DH:IKW])
                    o.then_inc(s_iwp, 1)
                if u in indexer_beside(g):
                    b, h = u // 8 + 1, u % 8
                    if u >= 2:
                        pe.wait_ge(s_rl, u - 1)
                    stacked_dots(PS[:, 4 + u % 2, 0:(b + 1) * P], b, h, 0).then_inc(s_dot, 1)

            def level(l):
                if l < len(LEVELS):
                    pe.wait_ge(s_Z, l + 1)
                if l == 0:
                    pe.wait_ge(s_iws, 1)
                for c in range(TB):
                    if l >= 1:
                        pe.wait_ge(s_ma, 4 * (l - 1) + c + 1)
                    for h in range(HEADS_A):
                        a = hb(Z[l % 2] if l < len(LEVELS) else kT, h)[:, c * P:(c + 1) * P]
                        b = hb(Z[l % 2] if l < len(LEVELS) else qT, h)[:, c * P:(c + 1) * P]
                        o = pe.matmul(PS[:, 4 + c, h * P:(h + 1) * P], a, b, start=True, stop=True)
                    o.then_inc(s_lvl, 1)

            def between_chunks():
                pe.wait_ge(s_Z, len(LEVELS) + 2)
                for i, (c, s) in enumerate(PAIRS):
                    if i < 4:
                        pe.wait_ge(s_ma, 4 * len(LEVELS) + i + 1)
                    else:
                        pe.wait_ge(s_ofs, i - 3)
                    for h in range(HEADS_A):
                        q = UX[:, h * P:(h + 1) * P] if c == 3 and s < 2 else hb(Z[1], h)[:, c * P:(c + 1) * P]
                        k = LX[:, h * P:(h + 1) * P] if c > 1 and s == 0 else hb(Z[0], h)[:, s * P:(s + 1) * P]
                        o = pe.matmul(PS[:, 4 + i % 4, h * P:(h + 1) * P], k, q, start=True, stop=True)
                    o.then_inc(s_off, 1)

            def recurrence_out():
                pe.wait_ge(s_ofs, len(PAIRS))
                pe.wait_ge(s_ma, 4 * (len(LEVELS) + 1))
                for g in range(4):
                    evacuated(pe, first_group["i"] + g)
                for c in range(TB):
                    for h in range(HEADS_A):
                        for s in range(c + 1):
                            S_t = Sd[:, c, :] if s == c else So[:, PAIRS.index((c, s)), :]
                            o = pe.matmul(PS[:, 4 + c, h * P:(h + 1) * P], S_t[:, h * P:(h + 1) * P],
                                          V[:, s * W + h * DK:s * W + (h + 1) * DK], start=(s == 0), stop=(s == c))
                    o.then_inc(s_o, 1)

            def turn_y():
                pe.wait_ge(s_yn, 1)
                for t in range(TB):
                    for h in range(HEADS_A):
                        o = pe.transpose(PS[:, 4 + t, h * P:(h + 1) * P],
                                         ya[:, t * W + h * DK:t * W + (h + 1) * DK], ident[:, :])
                    o.then_inc(s_yt, 1)

            pe.wait_ge(s_small, 64)
            pe.matmul(PS[0:HEADS_B, 0, :], tab, oh_sb[:, 0:S], start=True, stop=True)
            pe.matmul(PS[0:HEADS_B, 1, 0:P], tab, oh_sb[:, S:S + P], start=True, stop=True).then_inc(s_gps, 1)
            pe.wait_ge(s_const, 1)
            for t in range(TB):
                pe.wait_ge(s_hx, t + 1)
                if t == 3:
                    pe.wait_ge(s_hlo, 1)
                turn(xin[:, t, :], TURN_BANK[t])
            pe.wait_ge(s_gsb, 1)
            pe.wait_ge(s_lo, 1)
            pe.wait_ge(s_hlo, 2)
            for m in range(2):
                feature_group(weights(0), m, P, m, 0, S // 2, None)
            pe.wait_ge(s_hlo, TB)
            for m in range(2):
                feature_group(weights(0), m, P, m, S // 2, S, s_proj)
            for g in range(2, len(groups)):
                project(g)
                if g in LEVEL_AT:
                    level(LEVEL_AT[g])
                elif g == G_DIAG:
                    level(len(LEVELS))
                elif g == G_OFF:
                    between_chunks()
                elif g == G_REC:
                    recurrence_out()
                elif g == G_YTURN:
                    turn_y()
            for g in range(first_group["av"], len(groups)):
                evacuated(pe, g)
            def turn_y_b(b):
                pe.wait_ge(s_yb, b + 1)
                if b >= 2:
                    pe.wait_ge(s_ylo, b)
                for k in range(4):
                    o = pe.transpose(PS[:, 6 + b % 2, k * P:(k + 1) * P], yb[b % 2][:, k * P:(k + 1) * P], ident[:, :])
                o.then_inc(s_ybt, 1)

            for i in range(UNITS + PV_LAG):
                if i < UNITS:
                    b, h = divmod(i, HEADS_B)
                    if i >= 2:
                        pe.wait_ge(s_nm, i - 1)
                    stacked_dots(PS[:, i % 2, 0:(b + 1) * P], b, h, h).then_inc(s_qk, 1)
                if i >= PV_LAG:
                    u = i - PV_LAG
                    b, h = divmod(u, HEADS_B)
                    pe.wait_ge(s_pts[u % 2], u // 2 + 1)
                    if u == 0:
                        pe.wait_ge(s_yg, TB)
                    if h == 0 and b >= 2:
                        pe.wait_ge(s_yb, b - 1)
                    for s in range(b + 1):
                        o = pe.matmul(PS[:, 4 + b % 2, h * DH:(h + 1) * DH], PT[u % 2][:, s * P:(s + 1) * P],
                                      av[:, s * W + h * DH:s * W + (h + 1) * DH], start=(s == 0), stop=(s == b))
                    o.then_inc(s_pv, 1)
                if TURN_LAG <= i < UNITS + TURN_LAG:
                    u = i - TURN_LAG
                    pe.wait_ge(s_ex, u + 1)
                    if u >= 2:
                        pe.wait_ge(s_pts[u % 2], u // 2)
                    for s in range(u // HEADS_B + 1):
                        o = pe.transpose(PS[:, 2 + u % 2, s * P:(s + 1) * P], Pb[u % 4][:, s * P:(s + 1) * P],
                                         ident[:, :])
                    o.then_inc(s_ptp, 1)
                b = block_done(i - 2)
                if b is not None:
                    turn_y_b(b)

            def rows(j, k0, acts, order, first, last, done, before=None):
                w = weights(j)
                for t in order:
                    if before and t in before:
                        before[t]()
                    for kk in range(2):
                        k = k0 + kk
                        for half in range(2):
                            o = passes(k, [x[:, t * P:(t + 1) * P] for x in acts(k)],
                                       [x[:, kk, half * 512:(half + 1) * 512] for x in w],
                                       PS[:, 2 * t + half, :], first and kk == 0, last and kk == 1)
                    if last:
                        o.then_inc(done, 1)
                if not last:
                    o.then_inc(s_rows, 1)

            pe.wait_ge(s_ylo, 1)
            for c in range(KT // 2):
                pe.wait_ge(s_lo, J_WO + c + 1)
                before = {0: lambda: pe.wait_ge(s_nm, UNITS), 1: lambda: pe.wait_ge(s_pts[1], UNITS // 2),
                          2: lambda: turn_y_b(TB - 1), 3: lambda: pe.wait_ge(s_ylo, TB + 1)} if c == 0 else None
                rows(J_WO + c, 2 * c, lambda k: (hT_hi[:, k, :], hT_lo[:, k, :]), range(TB), c == 0,
                     c == KT // 2 - 1, s_wo, before)
            for t in range(TB):
                if t == 2:
                    pe.wait_ge(s_hlo, TB + 2)
                    pe.wait_ge(s_lo, J_FF + 1)
                    for m in range(2):
                        feature_group(weights(J_FF), m, P, m, 0, S // 2, None)
                pe.wait_ge(s_hx, TB + t + 1)
                turn(scr[t % 2], 2 * t)
            pe.wait_ge(s_hlo, 2 * TB)
            for j in range(J_FF, J_DN):
                c, up = divmod(j - J_FF, 2)
                pe.wait_ge(s_lo, j + 1)
                for m in range(2):
                    if c >= 1:
                        pe.wait_ge(s_fr, 2 * (c - 1) + m + 1)
                    feature_group(weights(j), m, P, 2 * up + m, S // 2 if j == J_FF else 0, S, s_gu)
            for c in range(FT // 2):
                pe.wait_ge(s_lo, J_DN + c + 1)
                pe.wait_ge(s_flo, 2 * c + 2)
                rows(J_DN + c, 2 * c, lambda k: (ff[:, k, 0, :], ff[:, k, 1, :]), (2, 3, 0, 1) if c == 0 else range(TB),
                     c == 0, c == FT // 2 - 1, s_dn, {0: lambda: pe.wait_ge(s_fr, FT)} if c == 0 else None)

    return nc


_INS = ['x', 'w_in', 'lb_logits', 'hgrn_gnorm', 'rel_bias', 'w_o', 'norm_pre_mix', 'norm_post_mix',
        'norm_pre_ffn', 'norm_post_ffn', 'w_gate', 'w_up', 'w_down']
_OUTS = [((1, 512, 1024), 'float32')]


def kernel(**inputs):
    import numpy as _np
    import concourse.bacc as _bacc
    from concourse import mybir as _mybir
    from concourse.bass_utils import run_bass_kernel_spmd as _run

    nc = _bacc.Bacc("TRN2", target_bir_lowering=False, num_devices=1)
    arrays, args = {}, []
    for name in _INS:
        a = _np.ascontiguousarray(inputs[name])
        arrays[f"in_{name}_dram"] = a
        args.append(nc.dram_tensor(f"in_{name}_dram", a.shape, _mybir.dt.from_np(a.dtype), kind="ExternalInput").ap())
    onehot = bucket_onehot(inputs["x"].shape[1])
    arrays["onehot_dram"] = onehot
    args.append(nc.dram_tensor("onehot_dram", onehot.shape, _mybir.dt.from_np(onehot.dtype),
                               kind="ExternalInput").ap())
    for i, (shape, dtype) in enumerate(_OUTS):
        dt = _mybir.dt.from_np(_np.dtype(dtype))
        args.append(nc.dram_tensor(f"out_{i}_dram", shape, dt, kind="ExternalOutput").ap())
    hymba_layer(nc, *args)
    r = _run(nc, [arrays], core_ids=[0])
    got = tuple(r.results[0][f"out_{i}_dram"] for i in range(len(_OUTS)))
    return got[0]
```

```python
from contextlib import ExitStack

import numpy as np

import concourse.bass as bass
from concourse import mybir

P = 128
F32 = mybir.dt.float32
F32R = mybir.dt.float32r
U32 = mybir.dt.uint32
ALU = mybir.AluOpType
ACT = mybir.ActivationFunctionType

HEADS_A, DK = 4, 128
HEADS_B, DH = 8, 64
TOPK_MAX = 256
N_BUCKETS, MAX_DISTANCE = 32, 128
EPS = 1e-6
FUTURE = -2.0e38
TAKEN = -3.0e38
CLOSED = -1.0e30


def bucket_onehot(seq):
    exact = N_BUCKETS // 2
    n = np.maximum(seq - 1 - np.arange(seq + P), 0)
    large = exact + (np.log(np.maximum(n, 1) / exact) / np.log(MAX_DISTANCE / exact)
                     * (N_BUCKETS - exact) + 1e-9).astype(np.int64)
    bucket = np.where(n < exact, n, np.minimum(large, N_BUCKETS - 1))
    return (np.arange(N_BUCKETS)[:, None] == bucket[None, :]).astype(np.float32)


def hymba_layer(nc, x, w_in, lb_logits, hgrn_gnorm, rel_bias, w_o, norm_pre_mix, norm_post_mix,
                norm_pre_ffn, norm_post_ffn, w_gate, w_up, w_down, onehot, out):
    _, S, D = x.shape
    F = w_gate.shape[2]
    TB = S // P
    KT = D // P
    FT = F // P
    W = HEADS_A * DK
    TOP = min(TOPK_MAX, S // 4)
    assert (S, D, W, TB, KT, FT, TOP) == (512, 1024, 512, 4, 8, 22, 128)
    CH = KT * 256

    x_d, out_d = x[0], out[0]
    wi, wo, wg, wu, wd = w_in[0], w_o[0], w_gate[0], w_up[0], w_down[0]
    gscr = nc.dram_tensor("bias_by_distance", [HEADS_B, P, S + P], F32, kind="Internal").ap()

    SEG = {"f": W, "q": 0, "i": 2 * W, "g": 3 * W, "aq": 4 * W, "ak": 5 * W, "av": 6 * W, "iq": 7 * W}
    chunks = [("iq", 0), ("iq", 1), ("ikw", 0)]
    chunks += [(s, c) for s in ("f", "q", "i", "av", "g", "aq", "ak") for c in range(2)]
    J_WO = len(chunks)
    chunks += [("wo", c) for c in range(KT // 2)]
    J_FF = len(chunks)
    for c in range(FT // 2):
        chunks += [("gate", c), ("up", c)]
    J_DN = len(chunks)
    chunks += [("down", c) for c in range(FT // 2)]
    NCH = len(chunks)
    IKW = DH + HEADS_B

    groups = []
    for j in range(J_WO):
        for m in range(1 if chunks[j][0] == "ikw" else 2):
            groups.append((j, chunks[j][0], chunks[j][1], m))
    first_group = {}
    for g, (j, kind, c, m) in enumerate(groups):
        first_group.setdefault(kind, g)

    LEVELS = [64, 32, 16, 8, 4, 2, 1]
    G_L0 = first_group["i"] + 1
    LEVEL_AT = {G_L0 + l: l for l in range(len(LEVELS))}
    G_DIAG = G_L0 + len(LEVELS)
    G_ENDS, G_OFF, G_REC, G_YNORM, G_YTURN, G_YGATE = (G_DIAG + n for n in (1, 2, 3, 5, 9, 10))
    PAIRS = [(c, s) for c in range(TB) for s in range(c)]
    G_TOPK = first_group["f"] + 2
    UNITS = TB * HEADS_B
    DOTS = (TB - 1) * HEADS_B
    TURN_LAG, PV_LAG = 3, 5
    TURN_BANK = (4, 6, 2, 4)

    with ExitStack() as ctx:
        def sb(name, shape, dt=F32):
            return ctx.enter_context(nc.sbuf_tensor(name, shape, dt))

        def sem(name):
            return ctx.enter_context(nc.semaphore(name))

        PS = ctx.enter_context(nc.psum_tensor("PS", [P, 8, 512], F32))

        hT_hi = sb("hT_hi", [P, KT, S], F32R)
        hT_lo = sb("hT_lo", [P, KT, S], F32R)
        raw = sb("raw", [P, 2, CH])
        w_hi = sb("w_hi", [P, 2, CH], F32R)
        w_lo = sb("w_lo", [P, 2, CH], F32R)
        ident = sb("ident", [P, P])
        lmask = sb("lmask", [P, len(LEVELS), 64])
        M0 = sb("M0", [P, P])
        iw = sb("iw", [P, TB, HEADS_B])
        ss = sb("ss", [P, 40])
        ms = sb("ms", [P, 40])
        rstd = sb("rstd", [P, 40])
        mhalf = sb("mhalf", [P, 16])
        lbt = sb("lbt", [P, 2, HEADS_A])
        lbw = sb("lbw", [P, 6, HEADS_A])
        gn = sb("gn", [P, 1])
        eB = sb("eB", [P, HEADS_A, TB])
        top8 = sb("top8", [P, 8])
        mx = sb("mx", [P, UNITS])
        nm = sb("nm", [P, UNITS])
        sm = sb("sm", [P, UNITS])
        rs = sb("rs", [P, UNITS])

        N1, N2 = FT * 2 * S, 7936
        low = ExitStack()
        A1 = low.enter_context(nc.sbuf_tensor("A1", [P, N1], F32))
        low.close()
        with ExitStack() as low:
            low.enter_context(nc.sbuf_tensor("A1_front", [P, 6144], F32))
            QK = low.enter_context(nc.sbuf_tensor("QK", [P, 3, HEADS_B, S], F32R))
        with ExitStack() as low:
            low.enter_context(nc.sbuf_tensor("A1_most", [P, 18432], F32))
            w_x = low.enter_context(nc.sbuf_tensor("w_x", [P, 2, CH], F32R))
        ff = sb("ff", [P, FT, 2, S], F32R)
        A2 = sb("A2", [P, N2])

        def a1(o, n):
            return A1[:, o:o + n]

        QS, QX, KS = QK[:, 0], QK[:, 1], QK[:, 2]
        gT, ya, av = a1(0, 2048), a1(2048, 2048), a1(4096, 2048)
        gain_in, iwT = a1(4096, 1024), a1(5120, 512)
        V = a1(6144, 2048)
        Z = [a1(8192, 2048), a1(10240, 2048)]
        Sd = a1(12288, 2048).rearrange("p (c n) -> p c n", c=TB)
        So = a1(14336, 3072).rearrange("p (i n) -> p i n", i=len(PAIRS))
        UX, LX = a1(17408, 512), a1(17920, 512)
        xin = a1(18432, 4096).rearrange("p (t d) -> p t d", t=TB)
        rl = [a1(18432, 512), a1(18944, 512)]
        BM = [a1(18432, 512), a1(18944, 512), a1(3072, 512)]
        QK_BANK = (0, 1, 7)
        Pb = [a1(19456 + 512 * i, 512) for i in range(4)]
        PT = [a1(21504 + 512 * i, 512) for i in range(2)]
        yb = [a1(2048, 512), a1(2560, 512)]
        scr = [a1(6144 + 1024 * i, 1024) for i in range(TB)]
        qT, kT = A2[:, 0:2048], A2[:, 2048:4096]
        x2 = A2[:, 0:4096].rearrange("p (t d) -> p t d", t=TB)
        bT = A2[:, 4096:6144]
        oh_sb, tab, g_sb = A2[0:N_BUCKETS, 4096:4736], A2[0:N_BUCKETS, 4736:4744], A2[0:HEADS_B, 4768:5408]
        gain_mid = A2[:, 4096:6144].rearrange("p (a d) -> p a d", a=2)
        sig = [A2[:, 4096:4608], A2[:, 4608:5120]]
        fraw = [A2[:, 5120:5632], A2[:, 5632:6144]]
        SC = {1: A2[:, 6144:6400], 2: A2[:, 6400:6784], 3: A2[:, 6784:7296]}
        gain_out = A2[:, 6144:7168]
        Bh = A2[:, 0:4096].rearrange("p (h c) -> p h c", h=HEADS_B)
        junk = a1(18432, 1024)
        junk_mid = a1(10240, 1024)

        s_x = [sem(f"x_landed{t}") for t in range(TB)]
        s_gin = sem("gain_in_landed")
        s_small = sem("small_landed")
        s_raw = [sem(f"raw_landed{i}") for i in range(2)]
        s_hi = sem("w_hi_ready")
        s_lo = sem("w_lo_ready")
        STACKED = [g for g in range(len(groups)) if groups[g][1] in ("iq", "ikw", "aq", "ak")]
        s_rows = sem("row_chunk_used")
        s_ss = sem("sumsq_ready")
        s_rs = sem("rstd_ready")
        s_pool = sem("pool_chain")
        s_dve = sem("dve_chain")
        s_const = sem("const_ready")
        s_hx = sem("h_ready")
        s_hps = sem("hT_psum")
        s_hhi = sem("hT_hi_ready")
        s_hlo = sem("hT_lo_ready")
        s_proj = sem("proj_done")
        s_ev = [sem(f"proj_evacuated{b}") for b in range(4)]
        s_sig = sem("silu_sigmoid_ready")
        s_lbm = sem("lb_max_sub")
        s_lbe = sem("lb_exp")
        s_gps = sem("bias_row_psum")
        s_gsb = sem("bias_row_sbuf")
        s_gst = sem("bias_row_stored")
        s_bh = sem("bias_tile_landed")
        s_sth = sem("stack_hi_ready")
        s_iwp = sem("w_idx_psum")
        s_iws = sem("w_idx_ready")
        s_dot = sem("idx_dots")
        s_rl = sem("idx_relu")
        s_sc = sem("idx_score")
        s_fut = sem("score_causal")
        s_mask = sem("mask_ready")
        s_f = sem("forget_ready")
        s_ln = sem("log_f_ready")
        s_b = sem("cumsum_ready")
        s_rst = sem("scan_reset_ready")
        s_D = sem("level_exponent")
        s_E = sem("level_exp")
        s_Z = sem("level_operands")
        s_lvl = sem("level_scores_psum")
        s_ma = sem("level_merged")
        s_eb = sem("chunk_decay")
        s_off = sem("offdiag_psum")
        s_ofs = sem("offdiag_sbuf")
        s_o = sem("hgrn_o_psum")
        s_half = sem("half_of_squares")
        s_ya = sem("hgrn_o_sbuf")
        s_yn = sem("hgrn_y_normed")
        s_yt = sem("hgrn_yT_psum")
        s_yg = sem("hgrn_yT_gated")
        s_bm = sem("bias_mask")
        s_qk = sem("logits_psum")
        s_nm = sem("neg_max")
        s_ex = sem("exp_done")
        s_ptp = sem("probsT_psum")
        s_pts = [sem("probsT_sbuf_even"), sem("probsT_sbuf_odd")]
        s_pv = sem("pv_done")
        s_yb = sem("attention_y_normed")
        s_ybt = sem("attention_yT_psum")
        s_yhi = sem("yT_hi_ready")
        s_ylo = sem("yT_lo_ready")
        s_mid = sem("x_and_gains_landed")
        s_wo = sem("mix_out_psum")
        s_x2 = sem("x2_ready")
        s_gu = sem("gate_up_psum")
        s_fs = sem("gate_sigmoid")
        s_fr = sem("ff_raw_ready")
        s_fhi = sem("ff_hi_ready")
        s_flo = sem("ff_lo_ready")
        s_go = sem("gain_out_landed")
        s_dn = sem("down_psum")
        s_fin = sem("final_ready")
        s_out = sem("out_stored")

        def hb(t, h):
            return t[:, h * S:(h + 1) * S]

        def block_done(i):
            b, h = divmod(i - PV_LAG, HEADS_B)
            return b if h == HEADS_B - 1 and 0 <= b < TB - 1 else None

        def indexer_beside(g):
            n = (g - first_group["f"]) * KT - 6
            return range(min(max(n, 0), DOTS), min(max(n + KT, 0), DOTS))

        def last_of_chunk(g):
            return g + 1 == len(groups) or groups[g + 1][0] != groups[g][0]

        def evacuated(eng, g):
            eng.wait_ge(s_ev[g % 4], g // 4 + 1)

        NORMS = [("in", t) for t in range(TB)] + [("hgrn", 0)]
        for t in range(TB):
            NORMS += [("mix", t), ("ffn", t)]
        NORMS += [("out", t) for t in range(TB)]

        def norm(kind, t):
            return NORMS.index((kind, t)) + 1

        def turned_to_sbuf(eng, u, copy):
            n = (u // 8 + 1) * P
            eng.wait_ge(s_ptp, u + 1)
            if u >= 2:
                eng.wait_ge(s_pv, u - 1)
            copy(PT[u % 2][:, 0:n], PS[:, 2 + u % 2, 0:n]).then_inc(s_pts[u % 2], 1)

        def used(eng, j):
            if j < J_WO:
                eng.wait_ge(s_proj, sum(g[0] <= j for g in groups))
            elif j < J_FF:
                eng.wait_ge(*((s_wo, TB) if j >= J_FF - 2 else (s_rows, j - J_WO + 1)))
            elif j < J_DN:
                eng.wait_ge(s_gu, 2 * (j - J_FF + 1))
            else:
                eng.wait_ge(s_rows, KT // 2 - 2 + j - J_DN + 1)

        def raw_src(j):
            kind, c = chunks[j]
            if kind == "ikw":
                return wi[:, 8 * W:8 * W + IKW].rearrange("(k p) n -> p k n", p=P)
            if kind in ("wo", "down"):
                src = wo if kind == "wo" else wd
                return src[c * 2 * P:(c + 1) * 2 * P, :].rearrange("(k p) n -> p k n", p=P)
            src = {"gate": wg, "up": wu}.get(kind, wi)
            lo = c * 256 + SEG.get(kind, 0)
            return src[:, lo:lo + 256].rearrange("(k p) n -> p k n", p=P)

        W_SLOT = {J_FF - 1: 2, J_FF: 0, J_FF + 1: 1, J_FF + 2: 2}

        def w_slot(j):
            return W_SLOT.get(j, j % 2)

        def slot_free(eng, j):
            before = [i for i in range(j) if w_slot(i) == w_slot(j)]
            if before:
                used(eng, before[-1])
            elif w_slot(j) == 2:
                eng.wait_ge(s_pv, UNITS)

        def w_split(j):
            if w_slot(j) == 2:
                return view(w_x[:, 0, :], j), view(w_x[:, 1, :], j)
            return view(w_hi[:, w_slot(j), :], j), view(w_lo[:, w_slot(j), :], j)

        def view(t, j):
            kind = chunks[j][0]
            if kind == "ikw":
                return t[:, 0:KT * IKW].rearrange("p (k n) -> p k n", k=KT)
            return t.rearrange("p (k n) -> p k n", k=2 if kind in ("wo", "down") else KT)

        def upper(t, z, c=None):
            return t.rearrange("p (n u z) -> p n u z", u=2, z=z)

        ctx.enter_context(nc.allow_non_contiguous_dma(reason="lower bounds and group gains go one per partition"))
        block = ctx.enter_context(nc.Block())

        @block.sync
        def _(sp):
            for t in range(TB):
                sp.dma_start(xin[:, t, :], x_d[t * P:(t + 1) * P, :]).then_inc(s_x[t], 16)
                if t == 0:
                    sp.dma_start(gain_in, norm_pre_mix[0, :].partition_broadcast(P)).then_inc(s_gin, 16)
            for j in range(NCH):
                if j >= 2:
                    sp.wait_ge(s_lo, j - 1)
                sp.dma_start(view(raw[:, j % 2, :], j), raw_src(j)).then_inc(s_raw[j % 2], 16)
            for t in range(TB):
                for half in range(2):
                    c = slice(half * 512, (half + 1) * 512)
                    sp.wait_ge(s_fin, 2 * t + half + 1)
                    sp.dma_start(out_d[t * P:(t + 1) * P, c], x2[:, t, c]).then_inc(s_out, 16)
            sp.wait_ge(s_out, 16 * 2 * TB)

        @block.gpsimd
        def _(pool):
            n_chain = [0]

            def link(ins):
                n_chain[0] += 1
                ins.then_inc(s_pool, 1)
                pool.wait_ge(s_pool, n_chain[0])

            def inv_root(col, n, width):
                link(pool.tensor_scalar(ms[:, col:col + n], ss[:, col:col + n], 1.0 / width, EPS, ALU.mult, ALU.add))
                pool.tensor_tensor(rstd[:, col:col + n], ms[:, col:col + n], mhalf[:, 0:n], ALU.pow).then_inc(s_rs, 1)

            link(pool.memset(ident[:, :], 0.0))
            pool.affine_select(out=ident[:, :], in_=ident[:, :], compare_op=ALU.not_equal, fill=1.0, base=0,
                               pattern=[[-1, P]], channel_multiplier=1).then_inc(s_const, 1)
            link(pool.memset(mhalf[:, :], -0.5))
            for t in range(TB):
                pool.wait_ge(s_ss, norm("in", t))
                inv_root(t, 1, D)
            link(pool.memset(lmask[:, :, :], 1.0))
            for l, z in enumerate(LEVELS):
                v = lmask[:, l, :].rearrange("p (n z) -> p n z", z=z)
                link(pool.affine_select(out=v, in_=v, compare_op=ALU.is_ge, fill=0.0, base=0,
                                        pattern=[[-2 * z, 64 // z], [0, z]], channel_multiplier=1))
                link(pool.affine_select(out=v, in_=v, compare_op=ALU.is_ge, fill=0.0, base=z - 1,
                                        pattern=[[2 * z, 64 // z], [0, z]], channel_multiplier=-1))
            link(pool.memset(M0[:, :], 0.0))
            pool.affine_select(out=M0[:, :], in_=M0[:, :], compare_op=ALU.is_ge, fill=CLOSED, base=0,
                               pattern=[[-1, P]], channel_multiplier=1).then_inc(s_const, 1)
            for b in (1, 2, 3):
                pool.wait_ge(s_sc, 8 * b)
                v = SC[b][:, b * P:(b + 1) * P]
                pool.affine_select(out=v, in_=v, compare_op=ALU.is_ge, fill=FUTURE, base=0,
                                   pattern=[[-1, P]], channel_multiplier=1).then_inc(s_fut, 1)
            pool.wait_ge(s_dot, DOTS)
            pool.memset(Sd[:, :, :], 0.0).then_inc(s_const, 1)
            link(pool.memset(Z[1], 1.0))
            pool.memset(Z[1].rearrange("p (n t) -> p n t", t=P)[:, :, 0:1], 0.0).then_inc(s_rst, 1)
            pool.wait_ge(s_b, 1)
            for l, z in enumerate(LEVELS):
                if l >= 2:
                    pool.wait_ge(s_lvl, 4 * (l - 1))
                b4 = upper(bT, z)
                d4 = upper(Z[l % 2], z)
                edge = b4[:, :, 0, z - 1:z].to_broadcast([P, S * HEADS_A // (2 * z), z])
                pool.tensor_tensor(d4[:, :, 1, :], b4[:, :, 1, :], edge, ALU.subtract)
                pool.tensor_tensor(d4[:, :, 0, :], edge, b4[:, :, 0, :], ALU.subtract).then_inc(s_D, 1)
            pool.wait_ge(s_lvl, 4 * len(LEVELS))
            b3 = bT.rearrange("p (n t) -> p n t", t=P)
            end = b3[:, :, P - 1:P].to_broadcast([P, HEADS_A * TB, P])
            pool.tensor_tensor(Z[0].rearrange("p (n t) -> p n t", t=P), end, b3, ALU.subtract).then_inc(s_D, 1)
            pool.wait_ge(s_gst, 16)
            pool.wait_ge(s_lvl, 4 * (len(LEVELS) + 1))
            pool.wait_ge(s_Z, len(LEVELS) + 2)
            for h in range(HEADS_B):
                pool.dma_start(Bh[:, h, :], bass.AP(tensor=gscr.tensor, offset=h * P * (S + P) + P - 1,
                                                    ap=[[S + P - 1, P], [1, S]])).then_inc(s_bh, 16)
            pool.wait_ge(s_E, len(LEVELS) + 2)
            pool.wait_ge(s_eb, 1)
            for a, gain in enumerate((norm_post_mix, norm_pre_ffn)):
                pool.dma_start(gain_mid[:, a, :], gain[0, :].partition_broadcast(P)).then_inc(s_mid, 16)
            pool.wait_ge(s_ss, norm("hgrn", 0))
            inv_root(16, 16, DK)
            pool.wait_ge(s_rs, norm("hgrn", 0))
            v = ya.rearrange("p (n d) -> p n d", d=DK)
            pool.tensor_tensor(v, v, rstd[:, 16:32].unsqueeze(2).to_broadcast([P, 16, DK]), ALU.mult).then_inc(s_yn, 1)
            pool.wait_ge(s_bh, 16 * HEADS_B)
            for u in range(UNITS):
                b, h = divmod(u, HEADS_B)
                n = (b + 1) * P
                if h == 0 and b:
                    pool.wait_ge(s_mask, b)
                if u == 2:
                    pool.wait_ge(s_yt, TB)
                if u >= 3:
                    pool.wait_ge(s_nm, u - 2)
                M = M0[:, :] if b == 0 else SC[b]
                pool.tensor_tensor(BM[u % 3][:, 0:n], Bh[:, h, (TB - 1 - b) * P:S], M, ALU.add).then_inc(s_bm, 1)
            pool.wait_ge(s_bm, UNITS)
            for t in range(TB):
                pool.dma_start(x2[:, t, :], x_d[t * P:(t + 1) * P, :]).then_inc(s_mid, 16)
            for k in range(TB):
                pool.wait_ge(s_ss, norm("mix", k))
                inv_root(4 + k, 1, D)
                pool.wait_ge(s_ss, norm("ffn", k))
                inv_root(8 + k, 1, D)
            pool.dma_start(gain_out, norm_post_ffn[0, :].partition_broadcast(P)).then_inc(s_go, 16)
            for t in range(TB):
                pool.wait_ge(s_ss, norm("out", t))
                inv_root(12 + t, 1, D)

        @block.scalar
        def _(act):
            def split(j):
                act.wait_ge(s_raw[j % 2], 16 * (j // 2 + 1))
                slot_free(act, j)
                act.activation(w_split(j)[0], view(raw[:, j % 2, :], j), ACT.Copy).then_inc(s_hi, 1)

            def turn_hi(n, banks, t):
                act.wait_ge(s_hps, n + 1)
                act.activation(hT_hi[:, :, t * P:(t + 1) * P],
                               PS[:, banks:banks + 2, :].rearrange("p a (k t) -> p (a k) t", t=P),
                               ACT.Copy).then_inc(s_hhi, 1)

            act.dma_start(lbt[:, :, :], lb_logits.rearrange("r (h p) -> p r h", p=P)).then_inc(s_small, 16)
            act.dma_start(gn[:, :], hgrn_gnorm.rearrange("a p -> p a")).then_inc(s_small, 16)
            act.dma_start(tab, rel_bias).then_inc(s_small, 16)
            act.dma_start(oh_sb, onehot).then_inc(s_small, 16)
            for t in range(TB):
                act.wait_ge(s_x[t], 16)
                if t:
                    act.wait_ge(s_ss, t)
                act.activation(ya[:, 0:D], xin[:, t, :], ACT.Square, accum_out=ss[:, t:t + 1]).then_inc(s_ss, 1)
            act.wait_ge(s_gps, 1)
            act.activation(g_sb[:, 0:S], PS[0:HEADS_B, 0, :], ACT.Copy)
            act.activation(g_sb[:, S:S + P], PS[0:HEADS_B, 1, 0:P], ACT.Copy).then_inc(s_gsb, 1)
            act.wait_ge(s_lbm, 1)
            act.activation(lbw[:, 1:3, :], lbt[:, :, :], ACT.Exp).then_inc(s_lbe, 1)
            for t in range(TB):
                turn_hi(t, TURN_BANK[t], t)
                if t == 1:
                    split(0)
            split(1)
            act.wait_ge(s_gsb, 1)
            act.dma_start(gscr, g_sb.unsqueeze(1).to_broadcast([HEADS_B, P, S + P])).then_inc(s_gst, 16)

            def evac(g):
                j, kind, c, m = groups[g]
                act.wait_ge(s_proj, g + 1)
                ps = PS[:, g % 4, :]
                done = s_ev[g % 4]
                h = 2 * c + m
                if kind in ("iq", "aq"):
                    if kind == "aq":
                        act.wait_ge(s_o, TB)
                    for e in range(2):
                        scale = DH ** -0.5 if kind == "aq" else 1.0
                        act.activation(QS[0:DH, 2 * h + e, :], ps[e * DH:(e + 1) * DH, :], ACT.Copy, scale=scale)
                        o = act.activation(QX[DH:P, 2 * h + e, :], ps[e * DH:(e + 1) * DH, :], ACT.Copy, scale=scale)
                    o.then_inc(s_sth, 1)
                elif kind == "ak":
                    for e in range(2):
                        o = act.activation(KS[0:DH, 2 * h + e, :], ps[e * DH:(e + 1) * DH, :], ACT.Copy)
                    o.then_inc(s_sth, 1)
                elif kind == "ikw":
                    act.wait_ge(s_hx, TB)
                    act.activation(KS[0:DH, 0, :], ps[0:DH, :], ACT.Copy)
                    act.activation(iwT[DH:IKW, :], ps[DH:IKW, :], ACT.Copy).then_inc(s_sth, 1)
                elif kind == "f":
                    if g == first_group["f"]:
                        act.wait_ge(s_gst, 16)
                    act.activation(hb(kT, h), ps, ACT.Sigmoid).then_inc(done, 1)
                elif kind in ("q", "g"):
                    act.activation(hb(qT if kind == "q" else gT, h), ps, ACT.Sigmoid).then_inc(s_sig, 1)
                else:
                    dst = (V if kind == "i" else av).rearrange("p (t n) -> p t n", t=TB)
                    act.activation(dst[:, 2 * m:2 * m + 2, c * 256:(c + 1) * 256],
                                   ps.rearrange("p (t n) -> p t n", t=2), ACT.Copy).then_inc(done, 1)

            def level_exp(l):
                act.wait_ge(s_D, l + 1)
                act.activation(Z[l % 2], Z[l % 2], ACT.Exp).then_inc(s_E, 1)

            for g, (j, kind, c, m) in enumerate(groups):
                if g in LEVEL_AT:
                    level_exp(LEVEL_AT[g])
                for u in indexer_beside(g):
                    n = (u // 8 + 2) * P
                    act.wait_ge(s_dot, u + 1)
                    if u >= 2:
                        act.wait_ge(s_sc, u - 1)
                    act.activation(rl[u % 2][:, 0:n], PS[:, 4 + u % 2, 0:n], ACT.Relu).then_inc(s_rl, 1)
                evac(g)
                if last_of_chunk(g) and j + 2 <= J_WO:
                    split(j + 2)
                if g == first_group["q"] - 1:
                    act.wait_ge(s_f, 1)
                    act.activation(Z[0], bT, ACT.Ln).then_inc(s_ln, 1)
                if g == G_DIAG:
                    b4 = bT.rearrange("p (h c t) -> p h c t", h=HEADS_A, c=TB)
                    act.activation(eB[:, :, :], b4[:, :, :, P - 1], ACT.Exp).then_inc(s_eb, 1)
                    act.wait_ge(s_lvl, 4 * (len(LEVELS) - 1))
                    act.activation(Z[1], bT, ACT.Exp).then_inc(s_E, 1)
                    act.wait_ge(s_D, len(LEVELS) + 1)
                    act.activation(Z[0], Z[0], ACT.Exp).then_inc(s_E, 1)
                if g == G_OFF:
                    for i in range(len(PAIRS)):
                        act.wait_ge(s_off, i + 1)
                        act.activation(So[:, i, :], PS[:, 4 + i % 4, :], ACT.Copy).then_inc(s_ofs, 1)
                if g == G_YNORM:
                    act.wait_ge(s_ya, TB)
                    for i in range(16):
                        if i == 8:
                            o.then_inc(s_half, 1)
                            act.wait_ge(s_half, 1)
                        o = act.activation(junk[:, i % 8 * DK:(i % 8 + 1) * DK], ya[:, i * DK:(i + 1) * DK],
                                           ACT.Square, accum_out=ss[:, 16 + i:17 + i])
                    o.then_inc(s_ss, 1)

            def y_hi_a(h):
                if h == 0:
                    act.wait_ge(s_yg, TB)
                    used(act, J_WO - 1)
                act.activation(hT_hi[:, h, :], hb(gT, h), ACT.Copy).then_inc(s_yhi, 1)

            def y_hi_b(b):
                act.wait_ge(s_ybt, b + 1)
                act.activation(hT_hi[:, 4:8, b * P:(b + 1) * P],
                               PS[:, 6, :].rearrange("p (k t) -> p k t", t=P), ACT.Copy).then_inc(s_yhi, 1)

            for i in range(UNITS + PV_LAG):
                if i < UNITS:
                    n = (i // 8 + 1) * P
                    act.wait_ge(s_nm, i + 1)
                    act.activation(Pb[i % 4][:, 0:n], Pb[i % 4][:, 0:n], ACT.Exp, bias=nm[:, i:i + 1],
                                   accum_out=sm[:, i:i + 1]).then_inc(s_ex, 1)
                if (i - TURN_LAG) % 2 == 0 and TURN_LAG <= i < UNITS + TURN_LAG:
                    turned_to_sbuf(act, i - TURN_LAG, lambda o, p: act.activation(o, p, ACT.Copy))
                if 2 <= i < 2 + HEADS_A:
                    y_hi_a(i - 2)
                b = block_done(i - 3)
                if b is not None:
                    y_hi_b(b)
            y_hi_b(TB - 1)
            split(J_WO + 1)
            split(J_WO + 2)
            split(J_WO + 3)
            split(J_WO + 4)

            def square_mix(k):
                act.wait_ge(s_wo, k + 1)
                act.wait_ge(s_ss, norm("mix", k) - 1)
                act.activation(junk_mid, PS[:, 2 * k:2 * k + 2, :].rearrange("p a n -> p (a n)"),
                               ACT.Square, accum_out=ss[:, 4 + k:5 + k]).then_inc(s_ss, 1)

            def square_x2(k):
                act.wait_ge(s_x2, k + 1)
                act.wait_ge(s_ss, norm("ffn", k) - 1)
                act.activation(junk_mid, x2[:, k, :], ACT.Square, accum_out=ss[:, 8 + k:9 + k]).then_inc(s_ss, 1)

            square_mix(0)
            square_x2(0)
            square_mix(1)
            square_x2(1)
            square_mix(2)
            turn_hi(TB, 0, 0)
            square_x2(2)
            turn_hi(TB + 1, 2, 1)
            square_mix(3)
            split(J_FF + 1)
            square_x2(3)
            turn_hi(TB + 2, 4, 2)
            turn_hi(TB + 3, 6, 3)
            for i in range(FT // 2):
                split(J_FF + 2 * i + 2)
                for f in (2 * i, 2 * i + 1):
                    act.wait_ge(s_gu, 2 * (f // 2) * 2 + (f % 2) + 1)
                    if f >= 2:
                        act.wait_ge(s_fr, f - 1)
                    act.activation(sig[f % 2], PS[:, f % 2, :], ACT.Sigmoid).then_inc(s_fs, 1)
                act.wait_ge(s_fr, 2 * i + 1)
                act.activation(ff[:, 2 * i, 0, :], fraw[0], ACT.Copy).then_inc(s_fhi, 1)
                split(J_FF + 2 * i + 3)
                act.wait_ge(s_fr, 2 * i + 2)
                act.activation(ff[:, 2 * i + 1, 0, :], fraw[1], ACT.Copy).then_inc(s_fhi, 1)
            for j in range(J_DN + 2, NCH):
                split(j)
            for t in range(TB):
                act.wait_ge(s_dn, t + 1)
                act.wait_ge(s_ss, norm("out", t) - 1)
                act.activation(raw[:, t % 2, 0:D], PS[:, 2 * t:2 * t + 2, :].rearrange("p a n -> p (a n)"),
                               ACT.Square, accum_out=ss[:, 12 + t:13 + t]).then_inc(s_ss, 1)

        @block.vector
        def _(dve):
            n_chain = [0]

            def link(ins):
                n_chain[0] += 1
                ins.then_inc(s_dve, 1)
                dve.wait_ge(s_dve, n_chain[0])

            def split(j):
                dve.wait_ge(s_hi, j + 1)
                hi, lo = w_split(j)
                dve.tensor_tensor(lo, view(raw[:, j % 2, :], j), hi.bitcast(F32), ALU.subtract).then_inc(s_lo, 1)

            def turn_lo(n, banks, t):
                dve.wait_ge(s_hhi, n + 1)
                dve.tensor_tensor(hT_lo[:, :, t * P:(t + 1) * P],
                                  PS[:, banks:banks + 2, :].rearrange("p a (k t) -> p (a k) t", t=P),
                                  hT_hi[:, :, t * P:(t + 1) * P].bitcast(F32), ALU.subtract).then_inc(s_hlo, 1)

            dve.wait_ge(s_small, 64)
            link(dve.tensor_tensor(lbw[:, 0, :], lbt[:, 0, :], lbt[:, 1, :], ALU.max))
            for r in range(2):
                o = dve.tensor_tensor(lbt[:, r, :], lbt[:, r, :], lbw[:, 0, :], ALU.subtract)
            o.then_inc(s_lbm, 1)
            dve.wait_ge(s_gin, 16)
            for t in range(TB):
                dve.wait_ge(s_rs, norm("in", t))
                dve.scalar_tensor_tensor(out=xin[:, t, :], in0=xin[:, t, :], scalar=rstd[:, t:t + 1], in1=gain_in,
                                         op0=ALU.mult, op1=ALU.mult).then_inc(s_hx, 1)
            for t in range(TB):
                turn_lo(t, TURN_BANK[t], t)
                if t == 1:
                    split(0)
            split(1)
            dve.wait_ge(s_lbe, 1)
            link(dve.tensor_tensor(lbw[:, 3, :], lbw[:, 1, :], lbw[:, 2, :], ALU.add))
            link(dve.reciprocal(lbw[:, 3, :], lbw[:, 3, :]))
            link(dve.tensor_tensor(lbw[:, 4, :], lbw[:, 1, :], lbw[:, 3, :], ALU.mult))
            link(dve.tensor_scalar(lbw[:, 5, :], lbw[:, 4, :], -1.0, 1.0, ALU.mult, ALU.add))

            def silu_mul(g):
                j, kind, c, m = groups[g]
                n_sig = g - first_group["q"] if kind == "q" else g - first_group["g"] + 4
                dve.wait_ge(s_sig, n_sig + 1)
                dst = hb(qT if kind == "q" else gT, 2 * c + m)
                dve.tensor_tensor(dst, PS[:, g % 4, :], dst, ALU.mult).then_inc(s_ev[g % 4], 1)

            def topk_round(r):
                b, k = r // 16 + 1, r % 16
                if k == 0:
                    dve.wait_ge(s_fut, b)
                link(dve.max(top8[:, :], SC[b]))
                link(dve.match_replace(SC[b], top8[:, :], SC[b], TAKEN))
                if k == 15:
                    dve.tensor_scalar(SC[b], SC[b], 0.5 * (FUTURE + TAKEN), CLOSED, ALU.is_gt,
                                      ALU.mult).then_inc(s_mask, 1)

            rounds = iter(range(48))

            def topk_rounds(n):
                for _, r in zip(range(n), rounds):
                    topk_round(r)

            def merge(l):
                z = LEVELS[l]
                if l:
                    dve.wait_ge(s_ma, 4 * l)
                for c in range(TB):
                    dve.wait_ge(s_lvl, 4 * l + c + 1)
                    v = Sd[:, c, :].rearrange("p (h n u z) -> p h n u z", h=HEADS_A, u=2, z=z)[:, :, :, 1, :]
                    s = PS[:, 4 + c, :].rearrange("p (h n u z) -> p h n u z", h=HEADS_A, u=2, z=z)[:, :, :, 1, :]
                    m = lmask[:, l, :].rearrange("p (n z) -> p n z", z=z).bitcast(U32)
                    m = m.unsqueeze(1).to_broadcast([P, HEADS_A, 64 // z, z])
                    dve.copy_predicated(v, m, s).then_inc(s_ma, 1)

            def chunk_ends():
                dve.wait_ge(s_E, len(LEVELS) + 1)
                link(dve.tensor_tensor(Z[1], Z[1], qT, ALU.mult))
                dve.wait_ge(s_E, len(LEVELS) + 2)
                link(dve.tensor_tensor(Z[0], Z[0], kT, ALU.mult))
                dve.wait_ge(s_eb, 1)
                for h in range(HEADS_A):
                    dve.tensor_scalar(UX[:, h * P:(h + 1) * P], hb(Z[1], h)[:, 3 * P:4 * P], eB[:, h, 2:3], None,
                                      ALU.mult)
                    o = dve.tensor_scalar(LX[:, h * P:(h + 1) * P], hb(Z[0], h)[:, 0:P], eB[:, h, 1:2], None,
                                          ALU.mult)
                o.then_inc(s_Z, 2)

            def diagonal():
                dve.wait_ge(s_ma, 4 * len(LEVELS))
                for c in range(TB):
                    dve.wait_ge(s_lvl, 4 * len(LEVELS) + c + 1)
                    dve.copy_predicated(Sd[:, c, :].rearrange("p (h t) -> p h t", t=P),
                                        ident[:, :].bitcast(U32).unsqueeze(1).to_broadcast([P, HEADS_A, P]),
                                        PS[:, 4 + c, :].rearrange("p (h t) -> p h t", t=P)).then_inc(s_ma, 1)

            def y_gate():
                for h in range(HEADS_A):
                    evacuated(dve, first_group["g"] + h)
                for t in range(TB):
                    dve.wait_ge(s_yt, t + 1)
                    v = gT.rearrange("p (h t) -> p h t", t=S)[:, :, t * P:(t + 1) * P]
                    dve.scalar_tensor_tensor(out=v, in0=PS[:, 4 + t, :].rearrange("p (h t) -> p h t", t=P),
                                             scalar=gn[:, 0:1], in1=v, op0=ALU.mult, op1=ALU.mult).then_inc(s_yg, 1)

            def stack_lo(g):
                j, kind, c, m = groups[g]
                dve.wait_ge(s_sth, STACKED.index(g) + 1)
                ps = PS[:, g % 4, :]
                h = 2 * c + m
                scale = DH ** -0.5 if kind == "aq" else 1.0
                for e in range(1 if kind == "ikw" else 2):
                    p, i = ps[e * DH:(e + 1) * DH, :], 0 if kind == "ikw" else 2 * h + e
                    if kind in ("iq", "aq"):
                        hi = (QX[DH:P, i, :] if e else QS[0:DH, i, :]).bitcast(F32)
                        outs = (QS[DH:P, i, :], QX[0:DH, i, :])
                    else:
                        hi, outs = KS[0:DH, i, :].bitcast(F32), (KS[DH:P, i, :],)
                    for t in outs:
                        o = dve.scalar_tensor_tensor(out=t, in0=p, scalar=scale, in1=hi, op0=ALU.mult,
                                                     op1=ALU.subtract)
                o.then_inc(s_ev[g % 4], 1)

            def evac(g):
                if g in STACKED:
                    stack_lo(g)
                elif groups[g][1] in ("q", "g"):
                    silu_mul(g)

            def level_operands(l):
                z = LEVELS[l]
                dve.wait_ge(s_E, l + 1)
                if l == 0:
                    for h in range(HEADS_A):
                        evacuated(dve, first_group["q"] + h)
                z4 = upper(Z[l % 2], z)
                dve.tensor_tensor(z4[:, :, 1, :], z4[:, :, 1, :], upper(qT, z)[:, :, 1, :], ALU.mult)
                dve.tensor_tensor(z4[:, :, 0, :], z4[:, :, 0, :], upper(kT, z)[:, :, 0, :],
                                  ALU.mult).then_inc(s_Z, 1)

            for g, (j, kind, _, m) in enumerate(groups):
                if g in LEVEL_AT:
                    level_operands(LEVEL_AT[g])
                if g == G_ENDS:
                    chunk_ends()
                if g == G_YGATE:
                    y_gate()
                for u in indexer_beside(g):
                    b, h = u // 8 + 1, u % 8
                    n = (b + 1) * P
                    if u == 0:
                        dve.wait_ge(s_iwp, 1)
                        dve.tensor_scalar(iw[:, :, :], PS[:, 6, 0:TB * HEADS_B].rearrange("p (t h) -> p t h", t=TB),
                                          HEADS_B ** -0.5 * DH ** -0.5, None, ALU.mult).then_inc(s_iws, 1)
                        dve.wait_ge(s_iws, 1)
                    dve.wait_ge(s_rl, u + 1)
                    if h == 0:
                        o = dve.tensor_scalar(SC[b], rl[u % 2][:, 0:n], iw[:, b, h:h + 1], None, ALU.mult)
                    else:
                        dve.wait_ge(s_sc, u)
                        o = dve.scalar_tensor_tensor(out=SC[b], in0=rl[u % 2][:, 0:n], scalar=iw[:, b, h:h + 1],
                                                     in1=SC[b], op0=ALU.mult, op1=ALU.add)
                    o.then_inc(s_sc, 1)
                evac(g)
                if g >= G_TOPK:
                    topk_rounds(2 if g < G_L0 - 4 or g > G_REC else 1)
                if g == first_group["q"] - 1:
                    for h in range(HEADS_A):
                        evacuated(dve, first_group["f"] + h)
                        o = dve.tensor_scalar(hb(bT, h), hb(kT, h), lbw[:, 5, h:h + 1], lbw[:, 4, h:h + 1],
                                              ALU.mult, ALU.add)
                    link(o)
                    dve.tensor_scalar(kT, bT, -1.0, 1.0, ALU.mult, ALU.add).then_inc(s_f, 1)
                elif g == first_group["q"] + 1:
                    dve.wait_ge(s_ln, 1)
                    dve.wait_ge(s_rst, 1)
                    dve.tensor_tensor_scan(bT, Z[1], Z[0], 0.0, ALU.mult, ALU.add).then_inc(s_b, 1)
                if g in LEVEL_AT:
                    if g == G_L0:
                        dve.wait_ge(s_const, 3)
                    merge(LEVEL_AT[g])
                elif g == G_DIAG:
                    diagonal()
                elif g == G_REC:
                    for c in range(TB):
                        dve.wait_ge(s_o, c + 1)
                        dve.tensor_copy(ya[:, c * W:(c + 1) * W], PS[:, 4 + c, :]).then_inc(s_ya, 1)
                if last_of_chunk(g) and j + 2 <= J_WO:
                    split(j + 2)
                if g >= G_TOPK:
                    topk_rounds(1)
            topk_rounds(48)

            def y_lo_a(h):
                dve.wait_ge(s_yhi, h + 1)
                dve.tensor_tensor(hT_lo[:, h, :], hb(gT, h), hT_hi[:, h, :].bitcast(F32), ALU.subtract).then_inc(s_ylo, 1)

            def y_lo_b(b):
                dve.wait_ge(s_yhi, HEADS_A + b + 1)
                dve.tensor_tensor(hT_lo[:, 4:8, b * P:(b + 1) * P],
                                  PS[:, 6, :].rearrange("p (k t) -> p k t", t=P),
                                  hT_hi[:, 4:8, b * P:(b + 1) * P].bitcast(F32), ALU.subtract).then_inc(s_ylo, 1)

            def y_norm_b(b):
                u = slice(8 * b, 8 * b + 8)
                dve.wait_ge(s_ex, 8 * b + 8)
                link(dve.reciprocal(rs[:, u], sm[:, u]))
                dve.wait_ge(s_pv, 8 * b + 8)
                if b >= 2:
                    dve.wait_ge(s_ybt, b - 1)
                dve.tensor_tensor(yb[b % 2].rearrange("p (h d) -> p h d", d=DH),
                                  PS[:, 4 + b % 2, :].rearrange("p (h d) -> p h d", d=DH),
                                  rs[:, u].unsqueeze(2).to_broadcast([P, HEADS_B, DH]), ALU.mult).then_inc(s_yb, 1)

            for i in range(UNITS + PV_LAG):
                if i < UNITS:
                    n = (i // 8 + 1) * P
                    dve.wait_ge(s_qk, i + 1)
                    dve.wait_ge(s_bm, i + 1)
                    if i >= 4:
                        dve.wait_ge(s_ptp, i - 3)
                    link(dve.tensor_tensor_reduce(Pb[i % 4][:, 0:n], PS[:, QK_BANK[i % 3], 0:n], BM[i % 3][:, 0:n], 1.0,
                                                  -3.4e38, ALU.add, ALU.max, mx[:, i:i + 1]))
                    dve.tensor_scalar(nm[:, i:i + 1], mx[:, i:i + 1], -1.0, None, ALU.mult).then_inc(s_nm, 1)
                if (i - TURN_LAG) % 2 == 1 and TURN_LAG <= i < UNITS + TURN_LAG:
                    turned_to_sbuf(dve, i - TURN_LAG, dve.tensor_copy)
                if 4 <= i < 4 + HEADS_A:
                    y_lo_a(i - 4)
                b = block_done(i - 1)
                if b is not None:
                    y_norm_b(b)
                b = block_done(i - 3)
                if b is not None:
                    y_lo_b(b)
            y_norm_b(TB - 1)
            y_lo_b(TB - 1)
            split(J_WO + 1)
            split(J_WO + 2)
            split(J_WO + 3)
            split(J_WO + 4)
            dve.wait_ge(s_mid, 16 * 6)

            def add_mix(k):
                dve.wait_ge(s_ss, norm("mix", k))
                link(dve.tensor_tensor(scr[k], PS[:, 2 * k:2 * k + 2, :].rearrange("p a n -> p (a n)"),
                                       gain_mid[:, 0, :], ALU.mult))
                dve.wait_ge(s_rs, norm("mix", k))
                dve.scalar_tensor_tensor(out=x2[:, k, :], in0=scr[k], scalar=rstd[:, 4 + k:5 + k],
                                         in1=x2[:, k, :], op0=ALU.mult, op1=ALU.add).then_inc(s_x2, 1)

            def norm_x2(k):
                dve.wait_ge(s_rs, norm("ffn", k))
                dve.wait_ge(s_x2, k + 1)
                dve.scalar_tensor_tensor(out=scr[k], in0=x2[:, k, :], scalar=rstd[:, 8 + k:9 + k],
                                         in1=gain_mid[:, 1, :], op0=ALU.mult, op1=ALU.mult).then_inc(s_hx, 1)

            add_mix(0)
            norm_x2(0)
            add_mix(1)
            norm_x2(1)
            add_mix(2)
            turn_lo(TB, 0, 0)
            norm_x2(2)
            turn_lo(TB + 1, 2, 1)
            add_mix(3)
            split(J_FF + 1)
            norm_x2(3)
            turn_lo(TB + 2, 4, 2)
            turn_lo(TB + 3, 6, 3)

            def ff_mul(f):
                dve.wait_ge(s_fs, f + 1)
                link(dve.tensor_tensor(sig[f % 2], PS[:, f % 2, :], sig[f % 2], ALU.mult))
                dve.wait_ge(s_gu, 4 * (f // 2) + 2 + f % 2 + 1)
                if f >= 2:
                    dve.wait_ge(s_fhi, f - 1)
                dve.tensor_tensor(fraw[f % 2], PS[:, 2 + f % 2, :], sig[f % 2], ALU.mult).then_inc(s_fr, 1)

            def ff_lo(f):
                dve.wait_ge(s_fhi, f + 1)
                dve.tensor_tensor(ff[:, f, 1, :], fraw[f % 2], ff[:, f, 0, :].bitcast(F32),
                                  ALU.subtract).then_inc(s_flo, 1)

            for i in range(FT // 2):
                split(J_FF + 2 * i + 2)
                ff_mul(2 * i)
                ff_lo(2 * i)
                ff_mul(2 * i + 1)
                split(J_FF + 2 * i + 3)
                ff_lo(2 * i + 1)
            for j in range(J_DN + 2, NCH):
                split(j)
            dve.wait_ge(s_go, 16)
            for t in range(TB):
                dve.wait_ge(s_ss, norm("out", t))
                o = raw[:, t % 2, D:2 * D]
                link(dve.tensor_tensor(o, PS[:, 2 * t:2 * t + 2, :].rearrange("p a n -> p (a n)"), gain_out, ALU.mult))
                dve.wait_ge(s_rs, norm("out", t))
                for half in range(2):
                    c = slice(half * 512, (half + 1) * 512)
                    dve.scalar_tensor_tensor(out=x2[:, t, c], in0=o[:, c], scalar=rstd[:, 12 + t:13 + t],
                                             in1=x2[:, t, c], op0=ALU.mult, op1=ALU.add).then_inc(s_fin, 1)

        @block.tensor
        def _(pe):
            def passes(k, lhs, rhs, out, first, last):
                for n, (a, b) in enumerate(((0, 1), (1, 0), (0, 0))):
                    o = pe.matmul(out, lhs[a], rhs[b], start=(first and n == 0), stop=(last and n == 2))
                return o

            def feature_group(w, m, M, bank, lo, hi, done, beside=None):
                for k in range(KT):
                    o = passes(k, [x[:, k, m * M:(m + 1) * M] for x in w],
                               [hT[:, k, lo:hi] for hT in (hT_hi, hT_lo)], PS[0:M, bank, lo:hi],
                               k == 0, k == KT - 1)
                    if k == KT - 1 and done is not None:
                        o.then_inc(done, 1)
                    if beside:
                        beside(k)

            def project(g):
                j, kind, _, m = groups[g]
                pe.wait_ge(s_lo, j + 1)
                w = w_split(j)
                if g >= 4:
                    evacuated(pe, g - 4)
                if kind in ("i", "av"):
                    for tt in range(2):
                        t = 2 * m + tt
                        for k in range(KT):
                            o = passes(k, [hT[:, k, t * P:(t + 1) * P] for hT in (hT_hi, hT_lo)],
                                       [x[:, k, :] for x in w], PS[:, g % 4, tt * 256:(tt + 1) * 256],
                                       k == 0, k == KT - 1)
                    o.then_inc(s_proj, 1)
                else:
                    feature_group(w, m, IKW if kind == "ikw" else P, g % 4, 0, S, s_proj,
                                  (lambda k: indexer_dot(g, k)) if len(indexer_beside(g)) else None)

            def turn(src, bank):
                for k in range(KT):
                    o = pe.transpose(PS[:, bank + k // 4, (k % 4) * P:(k % 4 + 1) * P],
                                     src[:, k * P:(k + 1) * P], ident[:, :])
                o.then_inc(s_hps, 1)

            def stacked_dots(out, b, h, kh):
                pe.matmul(out, QS[:, h, b * P:(b + 1) * P], KS[:, kh, 0:(b + 1) * P], start=True, stop=False)
                return pe.matmul(out, QX[:, h, b * P:(b + 1) * P], KS[:, kh, 0:(b + 1) * P], start=False, stop=True)

            def indexer_dot(g, k):
                u = (g - first_group["f"]) * KT + k - 6
                if u == 0:
                    evacuated(pe, first_group["ikw"])
                    for t in range(TB):
                        o = pe.transpose(PS[:, 6, t * HEADS_B:(t + 1) * HEADS_B], iwT[DH:IKW, t * P:(t + 1) * P],
                                         ident[DH:IKW, DH:IKW])
                    o.then_inc(s_iwp, 1)
                if u in indexer_beside(g):
                    b, h = u // 8 + 1, u % 8
                    if u >= 2:
                        pe.wait_ge(s_rl, u - 1)
                    stacked_dots(PS[:, 4 + u % 2, 0:(b + 1) * P], b, h, 0).then_inc(s_dot, 1)

            def level(l):
                if l < len(LEVELS):
                    pe.wait_ge(s_Z, l + 1)
                if l == 0:
                    pe.wait_ge(s_iws, 1)
                for c in range(TB):
                    if l >= 1:
                        pe.wait_ge(s_ma, 4 * (l - 1) + c + 1)
                    for h in range(HEADS_A):
                        a = hb(Z[l % 2] if l < len(LEVELS) else kT, h)[:, c * P:(c + 1) * P]
                        b = hb(Z[l % 2] if l < len(LEVELS) else qT, h)[:, c * P:(c + 1) * P]
                        o = pe.matmul(PS[:, 4 + c, h * P:(h + 1) * P], a, b, start=True, stop=True)
                    o.then_inc(s_lvl, 1)

            def between_chunks():
                pe.wait_ge(s_Z, len(LEVELS) + 2)
                for i, (c, s) in enumerate(PAIRS):
                    if i < 4:
                        pe.wait_ge(s_ma, 4 * len(LEVELS) + i + 1)
                    else:
                        pe.wait_ge(s_ofs, i - 3)
                    for h in range(HEADS_A):
                        q = UX[:, h * P:(h + 1) * P] if c == 3 and s < 2 else hb(Z[1], h)[:, c * P:(c + 1) * P]
                        k = LX[:, h * P:(h + 1) * P] if c > 1 and s == 0 else hb(Z[0], h)[:, s * P:(s + 1) * P]
                        o = pe.matmul(PS[:, 4 + i % 4, h * P:(h + 1) * P], k, q, start=True, stop=True)
                    o.then_inc(s_off, 1)

            def recurrence_out():
                pe.wait_ge(s_ofs, len(PAIRS))
                pe.wait_ge(s_ma, 4 * (len(LEVELS) + 1))
                for g in range(4):
                    evacuated(pe, first_group["i"] + g)
                for c in range(TB):
                    for h in range(HEADS_A):
                        for s in range(c + 1):
                            S_t = Sd[:, c, :] if s == c else So[:, PAIRS.index((c, s)), :]
                            o = pe.matmul(PS[:, 4 + c, h * P:(h + 1) * P], S_t[:, h * P:(h + 1) * P],
                                          V[:, s * W + h * DK:s * W + (h + 1) * DK], start=(s == 0), stop=(s == c))
                    o.then_inc(s_o, 1)

            def turn_y():
                pe.wait_ge(s_yn, 1)
                for t in range(TB):
                    for h in range(HEADS_A):
                        o = pe.transpose(PS[:, 4 + t, h * P:(h + 1) * P],
                                         ya[:, t * W + h * DK:t * W + (h + 1) * DK], ident[:, :])
                    o.then_inc(s_yt, 1)

            pe.wait_ge(s_small, 64)
            pe.matmul(PS[0:HEADS_B, 0, :], tab, oh_sb[:, 0:S], start=True, stop=True)
            pe.matmul(PS[0:HEADS_B, 1, 0:P], tab, oh_sb[:, S:S + P], start=True, stop=True).then_inc(s_gps, 1)
            pe.wait_ge(s_const, 1)
            for t in range(TB):
                pe.wait_ge(s_hx, t + 1)
                if t == 3:
                    pe.wait_ge(s_hlo, 1)
                turn(xin[:, t, :], TURN_BANK[t])
            pe.wait_ge(s_gsb, 1)
            pe.wait_ge(s_lo, 1)
            pe.wait_ge(s_hlo, 2)
            for m in range(2):
                feature_group(w_split(0), m, P, m, 0, S // 2, None)
            pe.wait_ge(s_hlo, TB)
            for m in range(2):
                feature_group(w_split(0), m, P, m, S // 2, S, s_proj)
            for g in range(2, len(groups)):
                project(g)
                if g in LEVEL_AT:
                    level(LEVEL_AT[g])
                elif g == G_DIAG:
                    level(len(LEVELS))
                elif g == G_OFF:
                    between_chunks()
                elif g == G_REC:
                    recurrence_out()
                elif g == G_YTURN:
                    turn_y()
            for g in range(first_group["av"], len(groups)):
                evacuated(pe, g)
            def turn_y_b(b):
                pe.wait_ge(s_yb, b + 1)
                if b >= 1:
                    pe.wait_ge(s_ylo, HEADS_A + b)
                for k in range(4):
                    o = pe.transpose(PS[:, 6, k * P:(k + 1) * P], yb[b % 2][:, k * P:(k + 1) * P], ident[:, :])
                o.then_inc(s_ybt, 1)

            for i in range(UNITS + PV_LAG):
                if i < UNITS:
                    b, h = divmod(i, HEADS_B)
                    if i == 2:
                        pe.wait_ge(s_yg, TB)
                    if i >= 3:
                        pe.wait_ge(s_nm, i - 2)
                    stacked_dots(PS[:, QK_BANK[i % 3], 0:(b + 1) * P], b, h, h).then_inc(s_qk, 1)
                if i >= PV_LAG:
                    u = i - PV_LAG
                    b, h = divmod(u, HEADS_B)
                    pe.wait_ge(s_pts[u % 2], u // 2 + 1)
                    if u == 0:
                        pe.wait_ge(s_yg, TB)
                    if h == 0 and b >= 2:
                        pe.wait_ge(s_yb, b - 1)
                    for s in range(b + 1):
                        o = pe.matmul(PS[:, 4 + b % 2, h * DH:(h + 1) * DH], PT[u % 2][:, s * P:(s + 1) * P],
                                      av[:, s * W + h * DH:s * W + (h + 1) * DH], start=(s == 0), stop=(s == b))
                    o.then_inc(s_pv, 1)
                if TURN_LAG <= i < UNITS + TURN_LAG:
                    u = i - TURN_LAG
                    pe.wait_ge(s_ex, u + 1)
                    if u >= 2:
                        pe.wait_ge(s_pts[u % 2], u // 2)
                    for s in range(u // HEADS_B + 1):
                        o = pe.transpose(PS[:, 2 + u % 2, s * P:(s + 1) * P], Pb[u % 4][:, s * P:(s + 1) * P],
                                         ident[:, :])
                    o.then_inc(s_ptp, 1)
                b = block_done(i - 2)
                if b is not None:
                    turn_y_b(b)

            def row_block(j, k0, acts, t, first, last):
                w = w_split(j)
                for kk in range(2):
                    k = k0 + kk
                    for half in range(2):
                        o = passes(k, [x[:, t * P:(t + 1) * P] for x in acts(k)],
                                   [x[:, kk, half * 512:(half + 1) * 512] for x in w],
                                   PS[:, 2 * t + half, :], first and kk == 0, last and kk == 1)
                return o

            pe.wait_ge(s_ylo, HEADS_A)
            def y_parts(k):
                return hT_hi[:, k, :], hT_lo[:, k, :]

            for c in range(KT // 2 - 2):
                pe.wait_ge(s_lo, J_WO + c + 1)
                for t in range(TB):
                    if c == 0 and t == 0:
                        pe.wait_ge(s_nm, UNITS)
                    elif c == 0 and t == 1:
                        pe.wait_ge(s_pts[0], UNITS // 2)
                        pe.wait_ge(s_pts[1], UNITS // 2)
                    elif c == 0 and t == 2:
                        turn_y_b(TB - 1)
                    elif c == 0 and t == 3:
                        pe.wait_ge(s_ylo, HEADS_A + TB)
                    o = row_block(J_WO + c, 2 * c, y_parts, t, c == 0, False)
                o.then_inc(s_rows, 1)
            pe.wait_ge(s_lo, J_FF)
            for t in range(TB):
                for c in (KT // 2 - 2, KT // 2 - 1):
                    if t == 3 and c == KT // 2 - 1:
                        pe.wait_ge(s_hx, TB + 2)
                        turn(scr[1], 2)
                    o = row_block(J_WO + c, 2 * c, y_parts, t, False, c == KT // 2 - 1)
                o.then_inc(s_wo, 1)
                if t == 2:
                    pe.wait_ge(s_hx, TB + 1)
                    turn(scr[0], 0)
            pe.wait_ge(s_hlo, TB + 2)
            pe.wait_ge(s_lo, J_FF + 1)
            for m in range(2):
                feature_group(w_split(J_FF), m, P, m, 0, S // 2, None)
            pe.wait_ge(s_hx, TB + 3)
            turn(scr[2], 4)
            pe.wait_ge(s_lo, J_FF + 2)
            for m in range(2):
                if m == 1:
                    pe.wait_ge(s_hx, TB + 4)
                    turn(scr[3], 6)
                feature_group(w_split(J_FF + 1), m, P, 2 + m, 0, S // 2, None)
            pe.wait_ge(s_hlo, 2 * TB)
            for j in range(J_FF, J_DN):
                c, up = divmod(j - J_FF, 2)
                pe.wait_ge(s_lo, j + 1)
                for m in range(2):
                    if c >= 1:
                        pe.wait_ge(s_fr, 2 * (c - 1) + m + 1)
                    feature_group(w_split(j), m, P, 2 * up + m, S // 2 if c == 0 else 0, S, s_gu)
            for c in range(FT // 2):
                pe.wait_ge(s_lo, J_DN + c + 1)
                pe.wait_ge(s_flo, 2 * c + 2)
                last = c == FT // 2 - 1
                for t in (2, 3, 0, 1) if c == 0 else range(TB):
                    if c == 0 and t == 0:
                        pe.wait_ge(s_fr, FT)
                    o = row_block(J_DN + c, 2 * c, lambda k: (ff[:, k, 0, :], ff[:, k, 1, :]), t, c == 0, last)
                    if last:
                        o.then_inc(s_dn, 1)
                if not last:
                    o.then_inc(s_rows, 1)

    return nc


_INS = ['x', 'w_in', 'lb_logits', 'hgrn_gnorm', 'rel_bias', 'w_o', 'norm_pre_mix', 'norm_post_mix',
        'norm_pre_ffn', 'norm_post_ffn', 'w_gate', 'w_up', 'w_down']
_OUTS = [((1, 512, 1024), 'float32')]


def kernel(**inputs):
    import numpy as _np
    import concourse.bacc as _bacc
    from concourse import mybir as _mybir
    from concourse.bass_utils import run_bass_kernel_spmd as _run

    nc = _bacc.Bacc("TRN2", target_bir_lowering=False, num_devices=1)
    arrays, args = {}, []
    for name in _INS:
        a = _np.ascontiguousarray(inputs[name])
        arrays[f"in_{name}_dram"] = a
        args.append(nc.dram_tensor(f"in_{name}_dram", a.shape, _mybir.dt.from_np(a.dtype), kind="ExternalInput").ap())
    onehot = bucket_onehot(inputs["x"].shape[1])
    arrays["onehot_dram"] = onehot
    args.append(nc.dram_tensor("onehot_dram", onehot.shape, _mybir.dt.from_np(onehot.dtype),
                               kind="ExternalInput").ap())
    for i, (shape, dtype) in enumerate(_OUTS):
        dt = _mybir.dt.from_np(_np.dtype(dtype))
        args.append(nc.dram_tensor(f"out_{i}_dram", shape, dt, kind="ExternalOutput").ap())
    hymba_layer(nc, *args)
    r = _run(nc, [arrays], core_ids=[0])
    got = tuple(r.results[0][f"out_{i}_dram"] for i in range(len(_OUTS)))
    return got[0]
```
